# Optimizing a Trainium2 kernel written in Bass

```python
import math
import jax, jax.numpy as jnp
from jax import lax
import numpy as np

D_MODEL = 2048
BATCH = 1
SEQ = 256
DEPTH = 1

GRID_W = 64
CTX_LEN = 256
N_MIXERS = 3
N_MOD = 6
MLP_HIDDEN = 4 * D_MODEL
NORM_EPS = 1e-6
FNET_GROUPS = 8
FNET_GROUP_DIM = D_MODEL // FNET_GROUPS
HGRN_EXPAND = 128
HGRN_HEADS = D_MODEL // HGRN_EXPAND
HGRN_DK = HGRN_EXPAND
HGRN_DV = D_MODEL // HGRN_HEADS
HGRN_F = HGRN_HEADS * HGRN_DK
HGRN_CHUNK = 16
DIFF_HEAD_DIM = 128
DIFF_HEADS = D_MODEL // (2 * DIFF_HEAD_DIM)
DIFF_V_DIM = 2 * DIFF_HEAD_DIM
Q_BLOCK = 128
ROPE_BASE = 10000.0


F32 = jnp.float32

def rms_norm(x, g):
    xf = x.astype(F32)
    y = xf * lax.rsqrt(jnp.mean(xf * xf, axis=-1, keepdims=True) + NORM_EPS)
    return (y * g.astype(F32)).astype(x.dtype)

def modulate(h, shift, scale):
    return h * (1 + scale) + shift

def sqrelu_mlp(h, w1, w2):
    return jnp.square(jax.nn.relu(h @ w1)) @ w2

def axial_rope_tables(n_tokens, dim):
    rows = n_tokens // GRID_W
    row = jnp.broadcast_to(jnp.arange(rows)[:, None], (rows, GRID_W)).reshape(-1).astype(F32)
    col = jnp.broadcast_to(jnp.arange(GRID_W)[None, :], (rows, GRID_W)).reshape(-1).astype(F32)
    n_freq = dim // 4
    inv = ROPE_BASE ** (-jnp.arange(n_freq, dtype=F32) / n_freq)
    ang = jnp.concatenate([row[:, None] * inv, col[:, None] * inv], axis=-1)
    return jnp.cos(ang), jnp.sin(ang)

def apply_rope(x, cos, sin):
    xf = x.astype(F32)
    x1, x2 = jnp.split(xf, 2, axis=-1)
    return jnp.concatenate([x1 * cos - x2 * sin, x1 * sin + x2 * cos], axis=-1).astype(x.dtype)

def fourier_mix(h):
    B, L, D = h.shape
    hg = h.astype(F32).reshape(B, L, FNET_GROUPS, FNET_GROUP_DIM)
    return jnp.fft.fftn(hg, axes=(1, 3)).real.reshape(B, L, D).astype(h.dtype)

def hgrn_lower_bounds(p):
    cs = jnp.cumsum(jax.nn.softmax(p.astype(F32), axis=0), axis=0)
    return cs - cs[0:1]

def chunk_gla(q, k, v, logf, s0):
    B, H, L, dk = q.shape
    C = HGRN_CHUNK
    N = L // C
    r = lambda t: jnp.moveaxis(t.astype(F32).reshape(B, H, N, C, t.shape[-1]), 2, 0)
    bcum = jnp.cumsum(logf.astype(F32).reshape(B, H, N, C, dk), axis=3)
    xs = (r(q), r(k), r(v), jnp.moveaxis(bcum, 2, 0))
    mask = jnp.tril(jnp.ones((C, C), dtype=bool))[:, :, None]

    def step(s, inp):
        qc, kc, vc, bc = inp
        bl = bc[:, :, -1:, :]
        decay = jnp.exp(jnp.where(mask, bc[:, :, :, None, :] - bc[:, :, None, :, :], -jnp.inf))
        a = jnp.einsum('bhtd,bhsd,bhtsd->bhts', qc, kc, decay)
        o = jnp.einsum('bhts,bhsv->bhtv', a, vc) + jnp.einsum('bhtd,bhdv->bhtv', qc * jnp.exp(bc), s)
        s = jnp.exp(bl[:, :, 0, :])[..., None] * s + jnp.einsum('bhsd,bhsv->bhdv', kc * jnp.exp(bl - bc), vc)
        return s, o

    s_final, o = lax.scan(step, s0.astype(F32), xs)
    return jnp.moveaxis(o, 0, 2).reshape(B, H, L, v.shape[-1]), s_final

def hgrn2_mixer(h_lat, h_ctx, w_in, lb, gnorm, w_out, ctx_out):
    lb = lb.reshape(2, HGRN_HEADS, HGRN_DK)

    def project(h):
        B, L, _ = h.shape
        q, zf, zb, v, g = jnp.split(h @ w_in, [HGRN_F, 2 * HGRN_F, 3 * HGRN_F, 3 * HGRN_F + D_MODEL], axis=-1)
        hd = lambda t: t.reshape(B, L, HGRN_HEADS, -1).transpose(0, 2, 1, 3)
        return hd(q), hd(zf), hd(zb), hd(v), hd(g)

    def forget(z, lbd):
        zf = z.astype(F32)
        l = lbd[None, :, None, :]
        logf = jnp.logaddexp(jnp.log(l), jnp.log1p(-l) + jax.nn.log_sigmoid(zf))
        key = (1 - l) * jax.nn.sigmoid(-zf)
        return logf, key

    def readout(o, g, dtype):
        B, H, L, _ = o.shape
        y = rms_norm(o, gnorm) * jax.nn.silu(g.astype(F32))
        return y.transpose(0, 2, 1, 3).reshape(B, L, H * HGRN_DV).astype(dtype) @ w_out

    flip = lambda t: jnp.flip(t, axis=2)
    qc, zfc, zbc, vc, gc = project(h_ctx)
    ql, zfl, zbl, vl, gl = project(h_lat)
    s0 = jnp.zeros((qc.shape[0], HGRN_HEADS, HGRN_DK, HGRN_DV), F32)
    lfc, kfc = forget(zfc, lb[0])
    o_cf, s_f = chunk_gla(qc, kfc, vc, lfc, s0)
    lfl, kfl = forget(zfl, lb[0])
    o_lf, _ = chunk_gla(ql, kfl, vl, lfl, s_f)
    lbc, kbc = forget(zbc, lb[1])
    o_cb, s_b = chunk_gla(flip(qc), flip(kbc), flip(vc), flip(lbc), s0)
    lbl, kbl = forget(zbl, lb[1])
    o_lb, _ = chunk_gla(flip(ql), flip(kbl), flip(vl), flip(lbl), s_b)
    y_lat = readout(o_lf + flip(o_lb), gl, h_lat.dtype)
    y_ctx = readout(o_cf + flip(o_cb), gc, h_ctx.dtype) if ctx_out else None
    return y_lat, y_ctx

def diff_core(q, k, v, lam):
    s = jnp.einsum('bhmqd,bhmkd->bhmqk', q, k).astype(F32) * (DIFF_HEAD_DIM ** -0.5)
    p = jax.nn.softmax(s, axis=-1)
    a = p[:, :, 0] - lam * p[:, :, 1]
    return jnp.einsum('bhqk,bhkv->bhqv', a.astype(v.dtype), v)

def diff_attention(h_lat, h_ctx, w_qkv, lam_p, subln, w_out, lambda_init, cos, sin, ctx_out):
    def project(h):
        B, L, _ = h.shape
        q, k, v = jnp.split(h @ w_qkv, 3, axis=-1)
        q = q.reshape(B, L, DIFF_HEADS, 2, DIFF_HEAD_DIM).transpose(0, 2, 3, 1, 4)
        k = k.reshape(B, L, DIFF_HEADS, 2, DIFF_HEAD_DIM).transpose(0, 2, 3, 1, 4)
        v = v.reshape(B, L, DIFF_HEADS, DIFF_V_DIM).transpose(0, 2, 1, 3)
        return q, k, v

    def merge(o, dtype):
        B, H, L, _ = o.shape
        o = rms_norm(o, subln) * (1 - lambda_init)
        return o.transpose(0, 2, 1, 3).reshape(B, L, H * DIFF_V_DIM).astype(dtype) @ w_out

    lp = lam_p.astype(F32)
    lam = jnp.exp(jnp.sum(lp[0] * lp[1])) - jnp.exp(jnp.sum(lp[2] * lp[3])) + lambda_init
    q_c, k_c, v_c = project(h_ctx)
    q_l, k_l, v_l = project(h_lat)
    q_l, k_l = apply_rope(q_l, cos, sin), apply_rope(k_l, cos, sin)
    k_all = jnp.concatenate([k_c, k_l], axis=3)
    v_all = jnp.concatenate([v_c, v_l], axis=2)
    B, H, _, L, d = q_l.shape
    nb = L // Q_BLOCK
    q_blocks = jnp.moveaxis(q_l.reshape(B, H, 2, nb, Q_BLOCK, d), 3, 0)
    o_blocks = lax.map(lambda qb: diff_core(qb, k_all, v_all, lam), q_blocks)
    o_l = jnp.moveaxis(o_blocks, 0, 2).reshape(B, H, L, DIFF_V_DIM)
    y_lat = merge(o_l, h_lat.dtype)
    y_ctx = merge(diff_core(q_c, k_c, v_c, lam), h_ctx.dtype) if ctx_out else None
    return y_lat, y_ctx

def first_inputs(seed: int = 0) -> dict:
    key = jax.random.key(seed)
    ks = jax.random.split(key, 20)
    n_slot = lambda m: len(range(m, DEPTH, N_MIXERS))
    n_a, n_b, n_c = n_slot(0), n_slot(1), n_slot(2)
    D = D_MODEL
    nrm = lambda k, shape, s: jax.random.normal(k, shape, F32) * s
    return {
        'x': nrm(ks[0], (BATCH, SEQ, D), 1.0),
        'c': nrm(ks[1], (BATCH, D), 1.0),
        'ctx': nrm(ks[2], (BATCH, CTX_LEN, D), 1.0),
        'c_ctx': nrm(ks[3], (D,), 1.0),
        'w_mod': nrm(ks[4], (DEPTH, D, N_MOD * D), D ** -0.5),
        'b_mod': nrm(ks[5], (DEPTH, N_MOD * D), 0.01),
        'norm_g': 1.0 + nrm(ks[6], (DEPTH, 4, D), 0.02),
        'w_mlp_in': nrm(ks[7], (DEPTH, D, MLP_HIDDEN), D ** -0.5),
        'w_mlp_out': nrm(ks[8], (DEPTH, MLP_HIDDEN, D), MLP_HIDDEN ** -0.5),
        'fnet_w_out': nrm(ks[9], (n_a, D, D), D ** -0.5),
        'hgrn_w_in': nrm(ks[10], (n_b, D, 3 * HGRN_F + 2 * D), D ** -0.5),
        'hgrn_lb': nrm(ks[11], (DEPTH, 2, HGRN_F), 0.1),
        'hgrn_gnorm': 1.0 + nrm(ks[12], (n_b, HGRN_DV), 0.02),
        'hgrn_w_out': nrm(ks[13], (n_b, D, D), D ** -0.5),
        'diff_w_qkv': nrm(ks[14], (n_c, D, 3 * D), D ** -0.5),
        'diff_lambda': nrm(ks[15], (n_c, 4, DIFF_HEAD_DIM), 0.1),
        'diff_subln': 1.0 + nrm(ks[16], (n_c, DIFF_V_DIM), 0.02),
        'diff_w_out': nrm(ks[17], (n_c, D, D), D ** -0.5),
    }

def first_block(x, c, ctx, c_ctx, w_mod, b_mod, norm_g, w_mlp_in, w_mlp_out, fnet_w_out, hgrn_w_in, hgrn_lb, hgrn_gnorm, hgrn_w_out, diff_w_qkv, diff_lambda, diff_subln, diff_w_out):
    L = x.shape[1]
    cos, sin = axial_rope_tables(L, DIFF_HEAD_DIM)
    lower_bounds = hgrn_lower_bounds(hgrn_lb)
    silu_c = jax.nn.silu(c)
    silu_cc = jax.nn.silu(c_ctx)
    for i in range(DEPTH):
        mixer, slot = i % N_MIXERS, i // N_MIXERS
        ctx_out = i < DEPTH - 1
        ctx_in = ctx_out or mixer != 0
        sh1, sc1, g1, sh2, sc2, g2 = jnp.split((silu_c @ w_mod[i] + b_mod[i])[:, None, :], N_MOD, axis=-1)
        h_lat = modulate(rms_norm(x, norm_g[i, 0]), sh1, sc1)
        h_ctx = None
        if ctx_in:
            csh1, csc1, cg1, csh2, csc2, cg2 = jnp.split(silu_cc @ w_mod[i] + b_mod[i], N_MOD, axis=-1)
            h_ctx = modulate(rms_norm(ctx, norm_g[i, 0]), csh1, csc1)
        if mixer == 0:
            y_lat = fourier_mix(h_lat) @ fnet_w_out[slot]
            y_ctx = fourier_mix(h_ctx) @ fnet_w_out[slot] if ctx_out else None
        elif mixer == 1:
            y_lat, y_ctx = hgrn2_mixer(h_lat, h_ctx, hgrn_w_in[slot], lower_bounds[i], hgrn_gnorm[slot], hgrn_w_out[slot], ctx_out)
        else:
            lambda_init = 0.8 - 0.6 * math.exp(-0.3 * i)
            y_lat, y_ctx = diff_attention(h_lat, h_ctx, diff_w_qkv[slot], diff_lambda[slot], diff_subln[slot], diff_w_out[slot], lambda_init, cos, sin, ctx_out)
        x = x + g1 * rms_norm(y_lat, norm_g[i, 1])
        x = x + g2 * rms_norm(sqrelu_mlp(modulate(rms_norm(x, norm_g[i, 2]), sh2, sc2), w_mlp_in[i], w_mlp_out[i]), norm_g[i, 3])
        if ctx_out:
            ctx = ctx + cg1 * rms_norm(y_ctx, norm_g[i, 1])
            ctx = ctx + cg2 * rms_norm(sqrelu_mlp(modulate(rms_norm(ctx, norm_g[i, 2]), csh2, csc2), w_mlp_in[i], w_mlp_out[i]), norm_g[i, 3])
    return x


HEAD_DIM = 128
D_MIX = D_MODEL
GLA_HEADS = D_MIX // 2 // HEAD_DIM
GLA_DK = HEAD_DIM // 2
GLA_DV = HEAD_DIM
GLA_RANK = 16
GLA_TAU = 16.0
GLA_CHUNK = 64
FOX_HEADS = D_MIX // 4 // HEAD_DIM
FOX_BLOCK = 128
MEM_HEADS = 4
MEM_TOKENS = 256
N_OUT_HEADS = GLA_HEADS + FOX_HEADS + MEM_HEADS
D_FF = 4 * D_MODEL
EPS = 1e-6


def _in_widths():
    return (
        GLA_HEADS * GLA_DK,
        GLA_HEADS * GLA_DK,
        GLA_HEADS * GLA_DV,
        GLA_HEADS * GLA_DV,
        GLA_RANK,
        FOX_HEADS * HEAD_DIM,
        FOX_HEADS * HEAD_DIM,
        FOX_HEADS * HEAD_DIM,
        FOX_HEADS * HEAD_DIM,
        FOX_HEADS,
        MEM_HEADS * HEAD_DIM,
        MEM_HEADS * HEAD_DIM,
    )

def _split_points():
    pts, acc = [], 0
    for w in _in_widths()[:-1]:
        acc += w
        pts.append(acc)
    return pts

def rms_norm_2(x, g):
    xf = x.astype(jnp.float32)
    y = xf * lax.rsqrt(jnp.mean(xf * xf, axis=-1, keepdims=True) + EPS)
    return (y * g.astype(jnp.float32)).astype(x.dtype)

def _heads(t, h):
    return t.reshape(t.shape[0], t.shape[1], h, -1).transpose(0, 2, 1, 3)

def gla_chunked(q, k, v, log_a):
    B, H, S, DK = q.shape
    DV = v.shape[-1]
    C = GLA_CHUNK
    n = S // C

    def to_chunks(t):
        return t.reshape(B, H, n, C, t.shape[-1]).transpose(2, 0, 1, 3, 4)

    qc = to_chunks(q * (DK ** -0.5))
    kc, vc, gc = to_chunks(k), to_chunks(v), to_chunks(log_a)
    causal = jnp.tril(jnp.ones((C, C), dtype=bool))[:, :, None]

    def step(state, xs):
        qi, ki, vi, gi = xs
        b = jnp.cumsum(gi.astype(jnp.float32), axis=2)
        inter = jnp.einsum('bhck,bhkv->bhcv', qi * jnp.exp(b), state)
        rel = b[:, :, :, None, :] - b[:, :, None, :, :]
        decay = jnp.exp(jnp.where(causal, rel, -jnp.inf))
        scores = jnp.einsum('bhik,bhijk,bhjk->bhij', qi.astype(jnp.float32), decay,
                            ki.astype(jnp.float32))
        intra = jnp.einsum('bhij,bhjv->bhiv', scores, vi.astype(jnp.float32))
        b_last = b[:, :, -1:, :]
        new_state = (jnp.exp(b_last[:, :, 0, :])[..., None] * state
                     + jnp.einsum('bhck,bhcv->bhkv', ki * jnp.exp(b_last - b),
                                  vi.astype(jnp.float32)))
        return new_state, inter + intra

    state0 = jnp.zeros((B, H, DK, DV), jnp.float32)
    _, out = lax.scan(step, state0, (qc, kc, vc, gc))
    return out.transpose(1, 2, 0, 3, 4).reshape(B, H, S, DV)

def forgetting_attention(q, k, v, log_f):
    B, H, S, D = q.shape
    scale = D ** -0.5
    c = jnp.cumsum(log_f.astype(jnp.float32), axis=-1)
    outs = []
    for i in range(S // FOX_BLOCK):
        q0, q1 = i * FOX_BLOCK, (i + 1) * FOX_BLOCK
        qb, kb, vb = q[:, :, q0:q1], k[:, :, :q1], v[:, :, :q1]
        logits = (jnp.einsum('bhqd,bhkd->bhqk', qb, kb).astype(jnp.float32) * scale
                  + c[:, :, q0:q1, None] - c[:, :, None, :q1])
        mask = (q0 + jnp.arange(FOX_BLOCK))[:, None] >= jnp.arange(q1)[None, :]
        p = jax.nn.softmax(jnp.where(mask, logits, -jnp.inf), axis=-1)
        outs.append(jnp.einsum('bhqk,bhkd->bhqd', p.astype(v.dtype), vb))
    return jnp.concatenate(outs, axis=2)

def second_inputs(seed: int = 0) -> dict:
    key = jax.random.key(seed)
    ks = jax.random.split(key, 20)
    n = jax.random.normal
    d_in = sum(_in_widths())
    return {
        "x": n(ks[0], (BATCH, SEQ, D_MODEL), jnp.float32),
        "mem": n(ks[1], (BATCH, MEM_TOKENS, D_MODEL), jnp.float32),
        "attn_norm_g": 1.0 + 0.02 * n(ks[2], (D_MODEL,), jnp.float32),
        "w_in": n(ks[3], (D_MODEL, d_in), jnp.float32) * D_MODEL ** -0.5,
        "gla_a_w2": n(ks[4], (GLA_RANK, GLA_HEADS * GLA_DK), jnp.float32) * GLA_RANK ** -0.5,
        "gla_a_b": 0.5 * n(ks[5], (GLA_HEADS * GLA_DK,), jnp.float32),
        "fox_f_b": 3.0 + 0.5 * n(ks[6], (FOX_HEADS,), jnp.float32),
        "fox_q_norm_g": 1.0 + 0.02 * n(ks[7], (HEAD_DIM,), jnp.float32),
        "fox_k_norm_g": 1.0 + 0.02 * n(ks[8], (HEAD_DIM,), jnp.float32),
        "mem_norm_g": 1.0 + 0.02 * n(ks[9], (D_MODEL,), jnp.float32),
        "w_mem_kv": n(ks[10], (D_MODEL, 2 * MEM_HEADS * HEAD_DIM), jnp.float32) * D_MODEL ** -0.5,
        "mem_q_norm_g": 1.0 + 0.02 * n(ks[11], (HEAD_DIM,), jnp.float32),
        "mem_k_norm_g": 1.0 + 0.02 * n(ks[12], (HEAD_DIM,), jnp.float32),
        "out_norm_g": 1.0 + 0.02 * n(ks[13], (N_OUT_HEADS * HEAD_DIM,), jnp.float32),
        "w_out": n(ks[14], (N_OUT_HEADS * HEAD_DIM, D_MODEL), jnp.float32) * (N_OUT_HEADS * HEAD_DIM) ** -0.5,
        "mlp_norm_g": 1.0 + 0.02 * n(ks[15], (D_MODEL,), jnp.float32),
        "w_up": n(ks[16], (D_MODEL, D_FF), jnp.float32) * D_MODEL ** -0.5,
        "w_down": n(ks[17], (D_FF, D_MODEL), jnp.float32) * D_FF ** -0.5,
    }

def second_block(x, mem, attn_norm_g, w_in, gla_a_w2, gla_a_b, fox_f_b, fox_q_norm_g,
              fox_k_norm_g, mem_norm_g, w_mem_kv, mem_q_norm_g, mem_k_norm_g,
              out_norm_g, w_out, mlp_norm_g, w_up, w_down):
    B, S, _ = x.shape
    h = x
    for _layer in range(DEPTH):
        xn = rms_norm_2(h, attn_norm_g)
        proj = xn @ w_in
        (gq, gk, gv, gg, ga, fq, fk, fv, fg, ff, mq, mg) = jnp.split(proj, _split_points(), axis=-1)

        log_a = jax.nn.log_sigmoid((ga @ gla_a_w2 + gla_a_b).astype(jnp.float32)) / GLA_TAU
        gla_o = gla_chunked(_heads(gq, GLA_HEADS), _heads(gk, GLA_HEADS),
                            _heads(gv, GLA_HEADS), _heads(log_a, GLA_HEADS))
        gla_o = gla_o.astype(x.dtype).transpose(0, 2, 1, 3)

        fq_h = rms_norm_2(_heads(fq, FOX_HEADS), fox_q_norm_g)
        fk_h = rms_norm_2(_heads(fk, FOX_HEADS), fox_k_norm_g)
        log_f = jax.nn.log_sigmoid((ff + fox_f_b).astype(jnp.float32)).transpose(0, 2, 1)
        fox_o = forgetting_attention(fq_h, fk_h, _heads(fv, FOX_HEADS), log_f)
        fox_o = fox_o.astype(x.dtype).transpose(0, 2, 1, 3)

        mn = rms_norm_2(mem, mem_norm_g)
        mk, mv = jnp.split(mn @ w_mem_kv, 2, axis=-1)
        mk = rms_norm_2(mk.reshape(B, mem.shape[1], MEM_HEADS, HEAD_DIM), mem_k_norm_g)
        mv = mv.reshape(B, mem.shape[1], MEM_HEADS, HEAD_DIM)
        mq_h = rms_norm_2(mq.reshape(B, S, MEM_HEADS, HEAD_DIM), mem_q_norm_g)
        m_logits = jnp.einsum('bshd,bmhd->bhsm', mq_h, mk).astype(jnp.float32) * HEAD_DIM ** -0.5
        m_p = jax.nn.softmax(m_logits, axis=-1)
        mem_o = jnp.einsum('bhsm,bmhd->bshd', m_p.astype(mv.dtype), mv)

        o = jnp.concatenate([gla_o, fox_o, mem_o], axis=2)
        o = rms_norm_2(o, out_norm_g.reshape(N_OUT_HEADS, HEAD_DIM)).reshape(B, S, -1)
        gate = jnp.concatenate([jax.nn.silu(gg), jax.nn.sigmoid(fg), jax.nn.sigmoid(mg)], axis=-1)
        h = h + (o * gate) @ w_out

        u = jax.nn.relu(rms_norm_2(h, mlp_norm_g) @ w_up)
        h = h + (u * u) @ w_down
    return h


def setup_inputs(seed=0):
    out = dict(first_inputs(seed))
    for name, value in second_inputs(seed + 1).items():
        if name != "x":
            out[name + "_2"] = value
    return out


def reference(
    x, c, ctx, c_ctx, w_mod, b_mod, norm_g, w_mlp_in, w_mlp_out, fnet_w_out, hgrn_w_in, hgrn_lb,
    hgrn_gnorm, hgrn_w_out, diff_w_qkv, diff_lambda, diff_subln, diff_w_out, mem_2,
    attn_norm_g_2, w_in_2, gla_a_w2_2, gla_a_b_2, fox_f_b_2, fox_q_norm_g_2, fox_k_norm_g_2,
    mem_norm_g_2, w_mem_kv_2, mem_q_norm_g_2, mem_k_norm_g_2, out_norm_g_2, w_out_2,
    mlp_norm_g_2, w_up_2, w_down_2,
):
    x = first_block(
        x, c, ctx, c_ctx, w_mod, b_mod, norm_g, w_mlp_in, w_mlp_out, fnet_w_out, hgrn_w_in,
        hgrn_lb, hgrn_gnorm, hgrn_w_out, diff_w_qkv, diff_lambda, diff_subln, diff_w_out,
    )
    return second_block(
        x, mem_2, attn_norm_g_2, w_in_2, gla_a_w2_2, gla_a_b_2, fox_f_b_2, fox_q_norm_g_2,
        fox_k_norm_g_2, mem_norm_g_2, w_mem_kv_2, mem_q_norm_g_2, mem_k_norm_g_2, out_norm_g_2,
        w_out_2, mlp_norm_g_2, w_up_2, w_down_2,
    )


_drawn_inputs = setup_inputs


def setup_inputs(seed=0):
    import zlib

    import numpy as np

    out = dict(_drawn_inputs(seed))
    spreads = {}
    factors = {'b_mod': 3.461,
     'attn_norm_g_2': 3.87,
     'fox_q_norm_g_2': 8.0,
     'fox_k_norm_g_2': 8.0,
     'mem_norm_g_2': 8.0,
     'mem_q_norm_g_2': 8.0,
     'mem_k_norm_g_2': 8.0,
     'out_norm_g_2': 6.7,
     'mlp_norm_g_2': 12.086}
    for name, (base, spread) in spreads.items():
        noise = np.random.default_rng([zlib.crc32(name.encode()), seed]).standard_normal(out[name].shape)
        drawn = base * np.exp(spread * noise) if base else spread * noise
        out[name] = __import__('jax').numpy.asarray(drawn.astype(out[name].dtype))
    for name, factor in factors.items():
        out[name] = (out[name] * factor).astype(out[name].dtype)
    return out
```

```python
from contextlib import ExitStack

import concourse.bass as bass
import numpy as np
from concourse import mybir

F32 = mybir.dt.float32
F32R = mybir.dt.float32r
U8 = mybir.dt.uint8
ALU = mybir.AluOpType
ACT = mybir.ActivationFunctionType
AX = mybir.AxisListType

P = 128
D = 2048
S = 256
HALVES = S // P
KT = D // P
FF = 4 * D
GC = 512
CH = 8
RAW = 4
QT = FF // D
GQ = D // GC
MODC = 1024
MODN = KT * D // MODC
EPS = 1e-6
NEG = -1e30
GLA_TAU = 16.0
LEVELS = (128, 64, 32, 16, 8, 4, 2, 1, 0)

W_IN = dict(gq=0, gk=512, gv=1024, gg=2048, ga=3072, fq=3088, fk=3600, fv=4112, fg=4624, ff=5136, mq=5140, mg=5652)
VROW = dict(c=0, ng0=16, ng2=32, attn=48, mem=64, mlp=80, out=96, gab=112, fqg=116, fkg=117, mqg=118, mkg=119)
VROWS = 120


def program(nc, x, c, w_mod, b_mod, norm_g, w_mlp_in, w_mlp_out, fnet_w_out, mem, attn_g, w_in, gla_w2, gla_b,
            fox_b, fox_qg, fox_kg, mem_g, w_mem_kv, mem_qg, mem_kg, out_g, w_out, mlp_g, w_up, w_down,
            k_ident, k_dft, k_mask, k_nsel, k_sel, k_levels, out):
    ctx = ExitStack()
    with ctx:
        sems = {}

        def sem(name):
            if name not in sems:
                sems[name] = ctx.enter_context(nc.semaphore(name))
            return sems[name]

        BASE = 16512
        KB = 1024
        O_RAW, O_WH, O_WL = 0, 16 * KB, 48 * KB
        O_H, O_XT, O_U, O_Y = 80 * KB, 96 * KB, 128 * KB, 160 * KB
        O_ACC0, O_ACC1, O_TMP, O_SLOT = 176 * KB, 184 * KB, 192 * KB, 196 * KB
        O_CONST = 200 * KB
        const_at = [O_CONST]

        def at(name, shape, dt, offset):
            return nc.alloc_sbuf_tensor_at(name, shape, dt, offset=BASE + offset)

        def const(name, shape, dt, size=4):
            n = int(np.prod(shape[1:])) * size
            t = at(name, shape, dt, const_at[0])
            const_at[0] += (n + 31) // 32 * 32
            assert const_at[0] <= 207 * KB + 800
            return t

        raw = at("raw", [P, RAW, MODC], F32, O_RAW)
        wh = at("wh", [P, CH, 2, GC], F32R, O_WH)
        wl = at("wl", [P, CH, 2, GC], F32R, O_WL)
        h = at("h", [P, HALVES, D], F32, O_H)
        xt = at("xt", [P, KT, 2, S], F32R, O_XT)
        u = at("u", [P, KT, 2, S], F32R, O_U)
        y = at("y", [P, HALVES, D], F32, O_Y)
        acc = [at(f"acc{i}", [P, D], F32, o) for i, o in enumerate((O_ACC0, O_ACC1))]
        tmp = at("tmp", [P, 4, S], F32, O_TMP)
        slot = at("slot", [P, MODC], F32, O_SLOT)
        xn = at("xn", [P, 2, HALVES, D], F32R, O_U)
        junk = at("junk", [P, D], F32, O_U)
        mkt = at("mkt", [P, 4, S], F32, O_Y)
        mksq = at("mksq", [P, 4, S], F32, O_Y + 4 * KB)
        mvt = at("mvt", [P, HALVES, GC], F32, O_Y + 8 * KB)
        pdft = at("pdft", [P, 2, 2, 2, 2 * S], F32R, O_Y)
        dft_raw = at("dft_raw", [P, 2, 2 * S], F32, O_ACC1)
        lmask_raw = at("lmask_raw", [P, 8 * P], F32, O_ACC1 + 4 * KB)
        dfth = at("dfth", [P, 2, 2 * S], F32R, O_TMP)
        dftl = at("dftl", [P, 2, 2 * S], F32R, O_SLOT)
        AU = O_U
        qg, kg, bg, eg, qd, kd, soff = (at(n, [P, 4, S], F32, AU + i * 4 * KB)
                                        for i, n in enumerate(("qg", "kg", "bg", "eg", "qd", "kd", "soff")))
        gat, ffz, fft, fc = (at(n, [64, S], F32, AU + (28 + i) * KB) for i, n in enumerate(("gat", "ffz", "fft", "fc")))
        wsh = at("wsh", [P, KT, 64], F32R, AU + 16 * KB)
        wsl = at("wsl", [P, KT, 64], F32R, AU + 20 * KB)
        osq = at("osq", [P, 8, S], F32, AU)
        fqsq, fksq = (at(n, [P, 4, S], F32, AU + o * KB) for n, o in (("fqsq", 8), ("fksq", 12)))
        pf = at("pf", [P, 8, S], F32, AU + 16 * KB)
        fosq = at("fosq", [P, 4, S], F32, AU + 16 * KB)
        pm = at("pm", [P, 8, S], F32, AU + 24 * KB)
        fq, fk, fv, mq = (at(n, [P, 4, S], F32, O_H + i * 4 * KB) for i, n in enumerate(("fq", "fk", "fv", "mq")))
        pt = at("pt", [P, 4, 2, S], F32, O_H)
        ot = at("ot", [P, KT, S], F32, O_Y)
        sd = at("sd", [P, 16, P], F32, O_Y + 8 * KB)
        gv = at("gv", [P, HALVES, 2 * GC], F32, O_ACC0)
        gt = at("gt", [P, 4, S], F32, O_ACC0)
        wsr = at("wsr", [P, KT, 64], F32, O_ACC1)
        w2 = at("w2", [16, GC], F32, O_ACC1 + 4 * KB)
        mk = at("mk", [P, 4, S], F32, O_ACC1)
        mv = at("mv", [P, HALVES, GC], F32, O_ACC1 + 4 * KB)
        mask = at("mask", [P, HALVES, S], F32, O_SLOT)
        nsel = at("nsel", [64, 4, P], F32, O_SLOT + 2 * KB)
        ident = const("ident", [P, P], F32)
        ones = const("ones", [P, P], F32)
        vrow = const("vrow", [P, P], F32)
        vt = const("vt", [P, VROWS], F32)
        lmask = const("lmask", [P, 8, P], U8, 1)
        sel = const("sel", [64, 4], F32)
        foxb = const("foxb", [64, 1], F32)
        eps = const("eps", [P, 1], F32)
        siluc, a1, na1, s1, a2, s2, vtmp = (const(n, [P, KT], F32)
                                            for n in ("siluc", "a1", "na1", "s1", "a2", "s2", "vtmp"))
        ssq = const("ssq", [P, HALVES, 4], F32)
        ssm, srt, rstd = (const(n, [P, HALVES], F32) for n in ("ssm", "srt", "rstd"))
        dc = const("dc", [P, 2], F32)
        mx, nmx, sm, rs = (const(n, [P, 8], F32) for n in ("mx", "nmx", "sm", "rs"))
        ps = ctx.enter_context(nc.psum_tensor("ps", [P, 8, 512], F32))
        mk_dram = nc.dram_tensor("mk_spill", [P, 4 * S], F32).ap()
        mv_dram = nc.dram_tensor("mv_spill", [P, HALVES * GC], F32).ap()
        h_dram = nc.dram_tensor("h_spill", [P, HALVES * D], F32).ap()

        def rows(w):
            return w.rearrange("(kt p) n -> p kt n", p=P)

        def flat(ap):
            return ap.rearrange("p a b -> p (a b)")

        def v(name, n=1, i=0):
            return vt[:, VROW[name] + i:VROW[name] + i + n]

        C_SC1 = 0
        C_MEM = C_SC1 + MODN
        C_SC2 = C_MEM + 2 * CH + MODN
        C_FN = C_SC2 + MODN
        C_SH2 = C_FN + GQ * CH + MODN
        C_ML1 = C_SH2 + MODN
        G_MEM, G_FN, G_ML1 = 0, 2, 2 + GQ
        G_WIN = G_ML1 + 2 * QT * GQ
        G_WO = G_WIN + 12
        G_ML2 = G_WO + GQ
        C_OFF = C_ML1 - CH * G_ML1

        def chunk_c(m):
            if m < CH * G_FN:
                return C_MEM + 3 * m
            if m < CH * G_ML1:
                return C_FN + 2 * (m - CH * G_FN)
            return m + C_OFF

        block = ctx.enter_context(nc.Block())

        @block.sync
        def _(sp):
            def load(cc, view, slots_used=1):
                s = cc % RAW
                if not isinstance(cc, int) or cc >= RAW:
                    sp.wait_ge(sem("raw_used"), cc - RAW + 1)
                sp.dma_start(raw_slot(s, view), view).then_inc(sem(f"raw_landed{s}"), 16)

            def raw_slot(s, view):
                return raw[:, s, :] if len(view.shape) == 2 else raw[:, s, :].rearrange("p (t n) -> p t n", t=2)

            def mod_view(vec, n):
                kt, half = divmod(n, 2)
                return w_mod[0, kt * P:(kt + 1) * P, vec * D + half * MODC:vec * D + (half + 1) * MODC]

            def weight(w, i, col):
                return rows(w)[:, 2 * i:2 * i + 2, col:col + GC]

            sp.dma_start(y[:, :, :], mem[0].rearrange("(a p) d -> p a d", p=P)).then_inc(sem("mem_in"), 16)
            sp.dma_start(h[:, :, :], x[0].rearrange("(a p) d -> p a d", p=P)).then_inc(sem("x_in"), 16)
            for n in range(MODN):
                load(C_SC1 + n, mod_view(1, n))
            for m in range(2 * CH):
                load(chunk_c(m), weight(w_mem_kv, m % CH, (m // CH) * GC))
                for j in range(2):
                    load(chunk_c(m) + 1 + j, mod_view(0, 2 * m + j))
            for n in range(MODN):
                load(C_SC2 + n, mod_view(4, n))
            for m in range(CH * G_FN, CH * G_ML1):
                n = m - CH * G_FN
                load(chunk_c(m), weight(fnet_w_out[0], n % CH, (n // CH) * GC))
                load(chunk_c(m) + 1, mod_view(2, n))
            for n in range(MODN):
                load(C_SH2 + n, mod_view(3, n))

            def ring_group(c0, view_of):
                for i in range(CH):
                    sp.wait_ge(sem("raw_used"), c0 + i - RAW + 1)
                    sp.dma_start(raw[:, i % RAW, :].rearrange("p (t n) -> p t n", t=2),
                                 view_of(i)).then_inc(sem(f"raw_landed{i % RAW}"), 16)

            def mlp_loads(G0, w1, w2_):
                c0 = CH * G0 + C_OFF
                with sp.Fori(0, QT) as q:
                    with sp.Fori(0, GQ) as g:
                        ring_group(c0 + 64 * q + 8 * g,
                                   lambda i: rows(w1)[:, 2 * i:2 * i + 2, bass.ds(q * D + g * GC, GC)])
                    with sp.Fori(0, GQ) as g:
                        ring_group(c0 + 32 + 64 * q + 8 * g,
                                   lambda i: rows(w2_)[:, bass.ds(q * KT + 2 * i, 2), bass.ds(g * GC, GC)])

            mlp_loads(G_ML1, w_mlp_in[0], w_mlp_out[0])
            for k, (name, off) in enumerate(WIN_GROUPS):
                ring_group(CH * (G_WIN + k) + C_OFF,
                           lambda i: rows(w_in)[:, 2 * i:2 * i + 2, W_IN[name] + off:W_IN[name] + off + GC])
            with sp.Fori(0, GQ) as g:
                ring_group(CH * G_WO + C_OFF + 8 * g,
                           lambda i: rows(w_out)[:, 2 * i:2 * i + 2, bass.ds(g * GC, GC)])
            mlp_loads(G_ML2, w_up, w_down)
            for n in range(4):
                a, b = divmod(n, 2)
                sp.wait_ge(sem("out_ready"), n + 1)
                sp.dma_start(out[0].rearrange("(a p) d -> p a d", p=P)[:, a, b * 1024:(b + 1) * 1024],
                             h[:, a, b * 1024:(b + 1) * 1024]).then_inc(sem("stored"), 16)
            sp.wait_ge(sem("stored"), 64)

        @block.gpsimd
        def _(pool):
            pool.memset(ones[:, :], 1.0).then_inc(sem("const_set"), 1)
            pool.memset(eps[:, :], EPS).then_inc(sem("const_set"), 1)

            def seed(n, vec):
                pool.memset(acc[n % 2][:, :], 0.0).then_inc(sem("acc_zero"), 1)
                pool.wait_ge(sem("acc_zero"), n + 1)
                pool.dma_start(acc[n % 2][0:1, :], b_mod[0:1, vec * D:(vec + 1) * D]).then_inc(sem(f"acc{n % 2}_seeded"), 16)

            def side_gain(k, row, half):
                pool.dma_start(slot[:, :], norm_g[0, row:row + 1, half * MODC:(half + 1) * MODC]
                               .to_broadcast([P, MODC])).then_inc(sem("slot_in"), 16)

            seed(0, 1)
            pool.wait_ge(sem("dft_lo"), 1)
            seed(1, 0)
            pool.wait_ge(sem("mod_out"), 1)
            seed(2, 4)
            pool.wait_ge(sem("mod_out"), 2)
            seed(3, 2)
            pool.wait_ge(sem("mod_out"), 3)
            seed(4, 3)
            pool.wait_ge(sem("dft_d"), 8)
            side_gain(0, 1, 0)
            pool.wait_ge(sem("slot_used"), 1)
            side_gain(1, 1, 1)
            pool.wait_ge(sem("mod_out"), 4)
            pool.memset(acc[0][:, :], 0.0).then_inc(sem("acc_zero"), 1)
            pool.wait_ge(sem("acc_zero"), 6)
            pool.dma_start(acc[0][0:1, :], b_mod[0:1, 5 * D:6 * D]).then_inc(sem("acc0_seeded"), 16)
            pool.wait_ge(sem("turned"), 8)
            pool.memset(y[:, :, :], 0.0).then_inc(sem("y_zero"), 1)
            with pool.Fori(0, QT * GQ) as n2:
                for half in range(2):
                    if half == 0:
                        pool.wait_ge(sem("slot_used"), n2 * 2 + 2)
                    else:
                        pool.wait_ge(sem("slot_used"), n2 * 2 + 3)
                    pool.dma_start(slot[:, :], rows(w_mod[0])[:, bass.ds(n2, 1), 5 * D + half * MODC:5 * D + (half + 1) * MODC]
                                   .rearrange("p a n -> p (a n)")).then_inc(sem("slot_in"), 16)
            pool.wait_ge(sem("h_piece"), 4)
            pool.memset(wsr[:, :, :], 0.0).then_inc(sem("wsr_zero"), 1)
            pool.wait_ge(sem("wsr_zero"), 1)
            pool.dma_start(wsr[:, :, 0:16], rows(w_in)[:, :, W_IN["ga"]:W_IN["ga"] + 16]).then_inc(sem("narrow_in"), 16)
            pool.dma_start(wsr[:, :, 32:36], rows(w_in)[:, :, W_IN["ff"]:W_IN["ff"] + 4]).then_inc(sem("narrow_in"), 16)
            pool.dma_start(w2[:, :], gla_w2).then_inc(sem("narrow_in"), 16)
            for half in range(2):
                if half == 0:
                    pool.wait_ge(sem("slot_used"), 2 + MODN)
                else:
                    pool.wait_ge(sem("slot_used"), 3 + MODN)
                side_gain(2 + half, 3, half)
            pool.wait_ge(sem("slot_used"), 4 + MODN)
            pool.dma_start(mask[:, :, :], k_mask.rearrange("p (a s) -> p a s", a=HALVES)).then_inc(sem("att_const"), 16)
            pool.dma_start(nsel[32:36, :, :], k_nsel.rearrange("p (a s) -> p a s", a=4)).then_inc(sem("att_const"), 16)
            pool.wait_ge(sem("h_piece"), 8)
            pool.dma_start(h_dram, flat(h[:, :, :])).then_inc(sem("h_spilled"), 16)
            pool.wait_ge(sem("la_mm"), 1)
            for t in (qd, kd, sd):
                pool.memset(t[:, :, :], 0.0).then_inc(sem("gla_zero"), 1)
            pool.wait_ge(sem("mkv_spilled"), 32)
            pool.dma_start(flat(mk[:, :, :]), mk_dram).then_inc(sem("mkv_in"), 16)
            pool.dma_start(flat(mv[:, :, :]), mv_dram).then_inc(sem("mkv_in"), 16)
            pool.wait_ge(sem("mem_pv"), 1)
            pool.wait_ge(sem("h_spilled"), 16)
            pool.dma_start(flat(h[:, :, :]), h_dram).then_inc(sem("h_back"), 16)
            pool.wait_ge(sem("turned"), 16)
            pool.memset(y[:, :, :], 0.0).then_inc(sem("y_zero"), 1)

        @block.tensor
        def _(pe):
            mm = nc.tensor.matmul

            def T_chunk(G, i, mlast, wide, c_wait, xt_wait=None):
                pe.wait_ge(sem("raw_used"), c_wait)
                par = G % 2
                for t in range(2):
                    kt = 2 * i + t
                    for j in range(4):
                        a, b = wh[:, i, t, j * P:(j + 1) * P], wl[:, i, t, j * P:(j + 1) * P]
                        first, end = kt == 0, kt == KT - 1
                        if wide:
                            o = ps[:, 4 * par + j, :]
                            mm(o, a, flat(xt[:, kt, :, :]), start=first, stop=end, skip_group_check=True)
                            last = mm(o[:, 0:S], b, xt[:, kt, 0, :], start=False, stop=end, skip_group_check=True)
                        else:
                            o = ps[:, 2 * par + j // 2, (j % 2) * S:(j % 2 + 1) * S]
                            mm(o, a, xt[:, kt, 0, :], start=first and j % 2 == 0, stop=False, skip_group_check=True)
                            mm(o, a, xt[:, kt, 1, :], start=False, stop=False, skip_group_check=True)
                            last = mm(o, b, xt[:, kt, 0, :], start=False, stop=end, skip_group_check=True)
                last.then_inc(sem("chunk_used"), 1)

            def N_chunk(G, i, act, wide, c_wait):
                pe.wait_ge(sem("raw_used"), c_wait)
                par = G % 2
                for t in range(2):
                    kt = 2 * i + t
                    for half in range(HALVES):
                        o = ps[:, (4 if wide else 2) * par + half, :]
                        hi, lo = (act[:, kt, z, half * P:(half + 1) * P] for z in range(2))
                        mm(o, hi, wh[:, i, t, :], start=kt == 0, stop=False, skip_group_check=True)
                        mm(o, hi, wl[:, i, t, :], start=False, stop=False, skip_group_check=True)
                        last = mm(o, lo, wh[:, i, t, :], start=False, stop=kt == KT - 1, skip_group_check=True)
                last.then_inc(sem("chunk_used"), 1)

            def bank_free(G):
                if not isinstance(G, int) or G >= 2:
                    pe.wait_ge(sem("evacuated"), G - 1)

            def transposes(build, src):
                for r in range(4):
                    if r >= 2:
                        pe.wait_ge(sem("xt_ready"), 4 * build + r - 1)
                    for j in range(4):
                        for half in range(HALVES):
                            kt = 4 * r + j
                            last = nc.tensor.transpose(
                                ps[:, 4 + 2 * (r % 2) + j // 2, (j % 2) * S + half * P:(j % 2) * S + (half + 1) * P],
                                src[:, half, kt * P:(kt + 1) * P], ident[:, :])
                    last.then_inc(sem("turned"), 1)

            pe.wait_ge(sem("consts_in"), 16 * N_CONSTS)
            nc.tensor.transpose(ps[:, 0, 0:VROWS], vrow[0:VROWS, :], ident[0:VROWS, 0:VROWS]).then_inc(sem("vt_mm"), 1)

            pe.wait_ge(sem("mem_normed"), 2)
            transposes(0, y)

            def mod_mm(n, a, c_end):
                pe.wait_ge(sem("raw_used"), c_end)
                if n:
                    pe.wait_ge(sem("mod_out"), n)
                for kt in range(KT):
                    last = mm(ps[:, 7, kt:kt + 1], acc[a][:, kt * P:(kt + 1) * P], ones[:, 0:1], start=True, stop=True)
                last.then_inc(sem("mod_mm"), 1)

            pe.wait_ge(sem("const_set"), 2)
            pe.wait_ge(sem("xt_ready"), 4)
            mod_mm(0, 0, C_MEM)
            for i in range(CH):
                if i % 2 == 0:
                    pe.wait_ge(sem("xt_ready"), 1 + i // 2)
                T_chunk(G_MEM, i, None, False, chunk_c(i) + 1)
            for i in range(CH):
                N_chunk(G_MEM + 1, i, xt, False, chunk_c(CH + i) + 1)
                if i == 3:
                    pe.wait_ge(sem("mksq_ready"), 1)
                    for n in range(2):
                        last = mm(ps[:, 4 + n, :], ones[:, :], flat(mksq[:, 2 * n:2 * n + 2, :]), start=True, stop=True)
                    last.then_inc(sem("mk_mm"), 1)
            mod_mm(1, 1, C_SC2)

            def dft_tokens(g):
                for dt in range(2):
                    if g >= 2:
                        pe.wait_ge(sem("p_lo"), g - 1)
                    o = ps[:, 4 + 2 * (g % 2) + dt, :]
                    d0 = (2 * g + dt) * P
                    for half in range(HALVES):
                        for z, t in ((0, dfth), (0, dftl), (1, dfth)):
                            last = mm(o, xn[:, z, half, d0:d0 + P], t[:, half, :], start=half == 0 and z == 0 and t is dfth,
                                      stop=half == 1 and z == 1, skip_group_check=True)
                last.then_inc(sem("dft_t"), 1)

            def dft_features(g):
                pe.wait_ge(sem("p_lo"), g + 1)
                if g >= 2:
                    pe.wait_ge(sem("fm_lo"), g - 1)
                for dq in range(2):
                    o = ps[:, g % 2, dq * S:(dq + 1) * S]
                    for kt in range(2):
                        for part in range(2):
                            lhs = slice(part * S + dq * P, part * S + (dq + 1) * P)
                            mv_ = slice(part * S, (part + 1) * S)
                            start = dq == 0 and kt == 0 and part == 0
                            mm(o, dfth[:, kt, lhs], pdft[:, g % 2, kt, 0, mv_], start=start, stop=False, skip_group_check=True)
                            mm(o, dftl[:, kt, lhs], pdft[:, g % 2, kt, 0, mv_], start=False, stop=False, skip_group_check=True)
                            last = mm(o, dfth[:, kt, lhs], pdft[:, g % 2, kt, 1, mv_], start=False,
                                      stop=kt == 1 and part == 1, skip_group_check=True)
                last.then_inc(sem("dft_d"), 1)

            pe.wait_ge(sem("xn_lo"), 2)
            pe.wait_ge(sem("dft_lo"), 1)
            pe.wait_ge(sem("mod_out"), 2)
            pe.wait_ge(sem("evacuated"), 2)
            dft_tokens(0)
            for g in range(8):
                if g < 7:
                    dft_tokens(g + 1)
                dft_features(g)
            mod_mm(2, 0, C_FN)

            for g in range(GQ):
                bank_free(G_FN + g)
                for i in range(CH):
                    if g == 0:
                        pe.wait_ge(sem("fm_lo"), i + 1)
                    N_chunk(G_FN + g, i, xt, False, chunk_c(CH * (G_FN + g) + i) + 1)

            def gate_rows(k, a):
                for n in range(4):
                    last = mm(ps[:, 4 + n, :], ones[:, :], acc[a][:, n * GC:(n + 1) * GC], start=True, stop=True)
                last.then_inc(sem("gate_mm"), 1)

            pe.wait_ge(sem("raw_used"), C_SH2)
            pe.wait_ge(sem("mod_out"), 3)
            gate_rows(0, 1)
            pe.wait_ge(sem("x_normed"), 2)
            pe.wait_ge(sem("slot_used"), 2)
            pe.wait_ge(sem("raw_used"), C_ML1)
            pe.wait_ge(sem("evacuated"), G_ML1)
            for kt in range(KT):
                last = mm(ps[:, 0, kt:kt + 1], acc[0][:, kt * P:(kt + 1) * P], ones[:, 0:1], start=True, stop=True)
            last.then_inc(sem("mod_mm"), 1)
            transposes(1, y)

            def mlp(G0, build, ups):
                c0 = CH * G0 + C_OFF
                with pe.Fori(0, QT) as q:
                    with pe.Fori(0, 2) as p:
                        for e in range(2):
                            pe.wait_ge(sem("evacuated"), q * 8 + p * 2 + (G0 + e - 1))
                            for i in range(CH):
                                if i % 2 == 0 and e == 0:
                                    pe.wait_ge(sem("xt_ready"), 4 * build + 1 + i // 2)
                                T_chunk(G0 + e, i, None, True, q * 64 + p * 16 + (c0 + 8 * e + i + 1))
                    with pe.Fori(0, 2) as p:
                        for e in range(2):
                            pe.wait_ge(sem("evacuated"), q * 8 + p * 2 + (G0 + 4 + e - 1))
                            for i in range(CH):
                                if i % 2 == 0 and e == 0:
                                    pe.wait_ge(sem("u_lo"), q * 4 + (ups + i // 2 + 1))
                                N_chunk(G0 + e, i, u, True, q * 64 + p * 16 + (c0 + 32 + 8 * e + i + 1))

            mlp(G_ML1, 1, 0)
            pe.wait_ge(sem("slot_used"), 2 + MODN)
            pe.wait_ge(sem("evacuated"), G_WIN)
            gate_rows(1, 0)
            pe.wait_ge(sem("x_normed"), 4)
            transposes(2, y)

            pe.wait_ge(sem("ws_lo"), 1)
            pe.wait_ge(sem("xt_ready"), 12)
            for kt in range(KT):
                for n, (w, z) in enumerate(((wsh, 0), (wsh, 1), (wsl, 0))):
                    last = mm(ps[0:64, 4, 0:S], w[:, kt, :], xt[:, kt, z, :], start=kt == 0 and n == 0,
                              stop=kt == KT - 1 and n == 2, skip_group_check=True)
            last.then_inc(sem("narrow_mm"), 1)

            def att_la():
                pe.wait_ge(sem("gat_ready"), 2)
                for j in range(4):
                    last = mm(ps[:, 4 + j // 2, (j % 2) * S:(j % 2 + 1) * S], w2[:, j * P:(j + 1) * P], gat[0:16, :],
                              start=True, stop=True)
                last.then_inc(sem("la_mm"), 1)

            def att_level(n):
                diag = LEVELS[n] == 0
                if diag:
                    pe.wait_ge(sem("lvl_out"), n)
                else:
                    pe.wait_ge(sem("lvl_ready"), n + 1)
                ka, qa = (kg, qg) if diag else (kd, qd)
                for hd in range(8):
                    o64 = 64 * (hd % 2)
                    for tb in range(1 if n == 0 else HALVES):
                        col = (4 * (hd % 2) + hd // 2 if n == 0 else 8 * (hd % 2) + 2 * (hd // 2) + tb) * P
                        i0 = P if n == 0 else tb * P
                        last = mm(ps[:, 4 + col // 512, col % 512:col % 512 + P],
                                  ka[o64:o64 + 64, hd // 2, tb * P:(tb + 1) * P],
                                  qa[o64:o64 + 64, hd // 2, i0:i0 + P], start=True, stop=True)
                last.then_inc(sem("lvl_mm"), 1)

            def att_gla_out():
                pe.wait_ge(sem("lvl_out"), len(LEVELS))
                for hd in range(8):
                    o = ps[:, 4 + hd // 2, (hd % 2) * S:(hd % 2 + 1) * S]
                    v0, v1 = (gv[:, a, hd * P:(hd + 1) * P] for a in range(2))
                    at0, off = 8 * (hd % 2) + 2 * (hd // 2), (4 * (hd % 2) + hd // 2) * P
                    mm(o[:, 0:P], v0, sd[:, at0, :], start=hd % 2 == 0, stop=True, skip_group_check=True)
                    mm(o[:, P:S], v0, flat(soff[:, :, :])[:, off:off + P], start=False, stop=False, skip_group_check=True)
                    last = mm(o[:, P:S], v1, sd[:, at0 + 1, :], start=False, stop=True, skip_group_check=True)
                last.then_inc(sem("gla_mm"), 1)

            def att_sums(name, n, sq, tiles, bank):
                pe.wait_ge(sem(name + "_sq"), n)
                for j in range(tiles // 2):
                    last = mm(ps[:, bank + j, :], ones[:, :], flat(sq[:, 2 * j:2 * j + 2, :]), start=True, stop=True)
                last.then_inc(sem(name + "_mm"), 1)

            def att_qk(name, qq, kk, fox):
                pe.wait_ge(sem(name + "_qk_ready"), 1)
                for hd in range(4):
                    for tb in range(HALVES):
                        o = ps[:, 4 + hd, tb * S:(tb + 1) * S]
                        last = mm(o, qq[:, hd, tb * P:(tb + 1) * P], kk[:, hd, :], start=tb == 0, stop=not fox,
                                  skip_group_check=True)
                        if fox:
                            mm(o, fc[32:36, tb * P:(tb + 1) * P], sel[32:36, hd:hd + 1].to_broadcast([4, S]),
                               start=False, stop=False, skip_group_check=True)
                            last = mm(o, nsel[32:36, hd, :], fc[32:36, :], start=False, stop=True, skip_group_check=True)
                last.then_inc(sem(name + "_qk"), 1)

            def att_turn(name, pr):
                pe.wait_ge(sem(name + "_p"), 1)
                for hd in range(4):
                    for tb in range(HALVES):
                        for sb_ in range(HALVES):
                            last = nc.tensor.transpose(ps[:, 4 + hd, sb_ * S + tb * P:sb_ * S + (tb + 1) * P],
                                                       pr[:, 2 * hd + tb, sb_ * P:(sb_ + 1) * P], ident[:, :])
                last.then_inc(sem(name + "_turn"), 1)

            def att_pv(name, val):
                pe.wait_ge(sem(name + "_pt"), 1)
                for hd in range(4):
                    for sb_ in range(HALVES):
                        last = mm(ps[:, 4 + hd // 2, (hd % 2) * S:(hd % 2 + 1) * S], val(sb_, hd), pt[:, hd, sb_, :],
                                  start=sb_ == 0 and hd % 2 == 0, stop=sb_ == 1, skip_group_check=True)
                last.then_inc(sem(name + "_pv"), 1)

            fvv = flat(fv[:, :, :]).rearrange("p (a n) -> p a n", a=HALVES)
            for k, (name, off) in enumerate(WIN_GROUPS):
                G = G_WIN + k
                bank_free(G)
                for i in range(CH):
                    cw = CH * G + C_OFF + i + 1
                    if name in ("gv", "fv"):
                        N_chunk(G, i, xt, False, cw)
                    else:
                        T_chunk(G, i, None, False, cw)
                    if (k, i) == (0, 3):
                        att_la()
                    if 2 <= k <= 6 and i == 3:
                        att_level(2 * (k - 2))
                    if 2 <= k <= 5 and i == 6:
                        att_level(2 * (k - 2) + 1)
                    if (k, i) == (6, 6):
                        att_gla_out()
                    if (k, i) == (7, 3):
                        att_sums("o", 1, osq, 8, 4)
                    if (k, i) == (7, 6):
                        pe.wait_ge(sem("o_root"), 1)
                        att_sums("fq", 1, fqsq, 4, 4)
                        att_sums("fk", 1, fksq, 4, 6)
                    if (k, i) == (8, 3):
                        pe.wait_ge(sem("att_const"), 32)
                        att_qk("fox", fq, fk, True)
                    if (k, i) == (8, 6):
                        att_turn("fox", pf)
                    if (k, i) == (9, 3):
                        att_pv("fox", lambda sb_, hd: fvv[:, sb_, hd * P:(hd + 1) * P])
                        att_sums("mq", 1, tmp, 4, 6)
                    if (k, i) == (9, 6):
                        att_sums("fo", 1, fosq, 4, 4)
                    if (k, i) == (10, 3):
                        pe.wait_ge(sem("mkv_in"), 32)
                        att_qk("mem", mq, mk, False)
                    if (k, i) == (10, 6):
                        att_turn("mem", pm)
                    if (k, i) == (11, 3):
                        att_pv("mem", lambda sb_, hd: mv[:, sb_, hd * P:(hd + 1) * P])
                    if (k, i) == (11, 6):
                        att_sums("mo", 1, tmp, 4, 6)

            with pe.Fori(0, 2) as p:
                for e in range(2):
                    pe.wait_ge(sem("evacuated"), p * 2 + (G_WO + e - 1))
                    for i in range(CH):
                        if i % 2 == 0 and e == 0:
                            pe.wait_ge(sem("z_lo"), i // 2 + 1)
                        N_chunk(G_WO + e, i, u, False, p * 16 + (CH * G_WO + C_OFF + 8 * e + i + 1))
            pe.wait_ge(sem("x_normed"), 6)
            transposes(3, y)
            mlp(G_ML2, 3, 16)

        @block.scalar
        def _(act):
            A = nc.scalar.activation
            v128 = lambda t: t.rearrange("(a p) -> a p", p=P)
            one = lambda t: t.rearrange("(a p) -> a p", a=1)
            col = lambda t: t.rearrange("(a o) -> a o", o=1)
            vec_rows = [("c", c[0], KT), ("ng0", norm_g[0, 0], KT), ("ng2", norm_g[0, 2], KT), ("attn", attn_g, KT),
                        ("mem", mem_g, KT), ("mlp", mlp_g, KT), ("out", out_g, KT), ("gab", gla_b, 4),
                        ("fqg", fox_qg, 1), ("fkg", fox_kg, 1), ("mqg", mem_qg, 1), ("mkg", mem_kg, 1)]
            consts = [(ident[:, :], k_ident)] + [(vrow[VROW[n]:VROW[n] + k, :], v128(t)) for n, t, k in vec_rows]
            consts += [(dft_raw[:, :, :], k_dft.rearrange("(a p) n -> p a n", p=P)),
                       (foxb[32:36, :], col(fox_b)), (sel[32:36, :], k_sel),
                       (lmask_raw[:, :], k_levels)]
            assert len(consts) == N_CONSTS
            for dst, src in consts:
                act.dma_start(dst, src).then_inc(sem("consts_in"), 16)

            def hi(i, landed, used):
                act.wait_ge(sem(f"raw_landed{landed[0]}"), landed[1])
                if used is not None:
                    act.wait_ge(sem("chunk_used"), used)
                A(flat(wh[:, i, :, :]), raw[:, landed[0], :], ACT.Copy).then_inc(sem("w_hi"), 1)

            def hi_static(m):
                cc = chunk_c(m)
                hi(m % CH, (cc % RAW, 16 * (cc // RAW + 1)), m - CH + 1 if m >= CH else None)

            def hi_run(m0):
                for j in range(CH):
                    i = (4 + j) % CH
                    hi(i, (j % RAW, (m0 + (C_OFF + RAW * (j // RAW) + RAW)) * 4), m0 + (j - CH + 1))

            def root(n):
                act.wait_ge(sem("ssm_ready"), n)
                A(srt[:, :], ssm[:, :], ACT.Sqrt, bias=eps[:, 0:1], scale=1.0 / D).then_inc(sem("rooted"), 1)

            def xt_hi(build, gain, shift=None):
                for r in range(4):
                    act.wait_ge(sem("turned"), 4 * build + r + 1)
                    for j in range(4):
                        src = ps[:, 4 + 2 * (r % 2) + j // 2, (j % 2) * S:(j % 2 + 1) * S]
                        kt = 4 * r + j
                        if shift is None:
                            last = A(xt[:, kt, 0, :], src, ACT.Copy, scale=gain[:, kt:kt + 1])
                        else:
                            last = A(xt[:, kt, 0, :], src, ACT.Identity, scale=gain[:, kt:kt + 1], bias=shift[:, kt:kt + 1])
                    last.then_inc(sem("xt_hi"), 1)

            act.wait_ge(sem("vt_ready"), 1)
            A(vtmp[:, :], v("c", KT), ACT.Exp, scale=-1.0).then_inc(sem("c_exp"), 1)
            act.wait_ge(sem("mem_in"), 16)
            act.wait_ge(sem("const_set"), 2)
            for a in range(HALVES):
                A(junk[:, :], y[:, a, :], ACT.Square, accum_out=ssq[:, a, 0:1]).then_inc(sem("sq"), 1)
                act.wait_ge(sem("sq"), a + 1)
            root(1)
            xt_hi(0, v("mem", KT))
            act.wait_ge(sem("x_in"), 16)
            act.wait_ge(sem("rs_ready"), 1)
            for a in range(HALVES):
                A(junk[:, :], h[:, a, :], ACT.Square, accum_out=ssq[:, a, 0:1]).then_inc(sem("sq"), 1)
                act.wait_ge(sem("sq"), 3 + a)
            root(2)
            act.wait_ge(sem("consts_in"), 16 * N_CONSTS)
            A(dfth[:, :, :], dft_raw[:, :, :], ACT.Copy).then_inc(sem("dft_hi"), 1)
            act.wait_ge(sem("rs_ready"), 2)
            for a in range(HALVES):
                A(xn[:, 0, a, :], h[:, a, :], ACT.Copy, scale=rstd[:, a:a + 1]).then_inc(sem("xn_hi"), 1)
            for m in range(CH + 4):
                hi_static(m)
            act.wait_ge(sem("evacuated"), 1)
            A(mksq[:, :, :], mkt[:, :, :], ACT.Square).then_inc(sem("mksq_ready"), 1)
            for m in range(CH + 4, 2 * CH):
                hi_static(m)
            act.wait_ge(sem("mk_mm"), 1)
            A(flat(mksq[:, :, :]).rearrange("p (b n) -> p b n", b=2), ps[:, 4:6, :], ACT.Sqrt, bias=eps[:, 0:1],
              scale=1.0 / P).then_inc(sem("mk_root"), 1)
            act.wait_ge(sem("mk_normed"), 1)
            act.dma_start(mk_dram, flat(mkt[:, :, :])).then_inc(sem("mkv_spilled"), 16)
            act.wait_ge(sem("evacuated"), 2)
            act.dma_start(mv_dram, flat(mvt[:, :, :])).then_inc(sem("mkv_spilled"), 16)
            act.wait_ge(sem("mkv_spilled"), 32)
            act.wait_ge(sem("a1_ready"), 2)

            def p_hi(g):
                act.wait_ge(sem("dft_t"), g + 1)
                if g >= 2:
                    act.wait_ge(sem("dft_d"), g - 1)
                for dt in range(2):
                    kt = 2 * g + dt
                    src = ps[:, 4 + 2 * (g % 2) + dt, :]
                    A(pdft[:, g % 2, dt, 0, 1:S], src[:, 1:S], ACT.Identity, scale=a1[:, kt:kt + 1])
                    last = A(pdft[:, g % 2, dt, 0, S:2 * S], src[:, S:2 * S], ACT.Identity, scale=na1[:, kt:kt + 1])
                last.then_inc(sem("p_hi"), 1)
                act.wait_ge(sem("dc_ready"), g + 1)
                A(pdft[:, g % 2, :, 0, 0:1].rearrange("p a b -> p (a b)"), dc[:, :], ACT.Copy).then_inc(sem("dc_hi"), 1)

            def fm_hi(g):
                act.wait_ge(sem("dft_d"), g + 1)
                A(xt[:, 2 * g:2 * g + 2, 0, :], ps[:, g % 2, :].rearrange("p (a b) -> p a b", a=2),
                  ACT.Copy).then_inc(sem("fm_hi"), 1)

            p_hi(0)
            for g in range(8):
                if g < 7:
                    p_hi(g + 1)
                fm_hi(g)
            for g in range(GQ):
                for m in range(CH * (G_FN + g) + (4 if g else 0), CH * (G_FN + g + 1) + (4 if g < GQ - 1 else 0)):
                    hi_static(m)
                act.wait_ge(sem("evacuated"), G_FN + g + 1)
                for a in range(HALVES):
                    A(tmp[:, 0:2, :].rearrange("p a b -> p (a b)"), y[:, a, g * GC:(g + 1) * GC], ACT.Square,
                      accum_out=ssq[:, a, g:g + 1]).then_inc(sem("sq"), 1)
                    act.wait_ge(sem("sq"), 5 + 2 * g + a)
            root(3)

            def h_squares(n0):
                for n in range(4):
                    a, b = divmod(n, 2)
                    act.wait_ge(sem("h_piece"), n0 + n + 1)
                    A(flat(tmp[:, :, :]), h[:, a, b * 1024:(b + 1) * 1024], ACT.Square,
                      accum_out=ssq[:, a, b:b + 1]).then_inc(sem("hsq"), 1)
                    act.wait_ge(sem("hsq"), n0 + n + 1)

            h_squares(0)
            root(4)
            for i in range(4):
                hi_static(CH * G_ML1 + i)
            act.wait_ge(sem("a2_ready"), 2)
            xt_hi(1, a2, s2)

            def mlp_quarter(G0, ups, q, last=False):
                with act.Fori(0, 2) as p:
                    for e in range(2):
                        hi_run(q * 64 + p * 16 + (CH * (G0 + e) + 4))
                        act.wait_ge(sem("chunk_used"), q * 64 + p * 16 + CH * (G0 + e + 1))
                        b0 = 4 * ((G0 + e) % 2)
                        A(tmp[:, :, :], ps[:, b0:b0 + 4, S:2 * S], ACT.Copy).then_inc(sem("up_lo"), 1)
                        act.wait_ge(sem("up_sq"), q * 4 + p * 2 + (ups + e + 1))
                        A(u[:, bass.ds(p * 8 + 4 * e, 4), 0, :], tmp[:, :, :], ACT.Copy).then_inc(sem("u_hi"), 1)

                def down(p, e, final=False):
                    m0 = q * 64 + p * 16 + (CH * (G0 + 4 + e) + 4)
                    if final:
                        for j in range(4):
                            hi(4 + j, (j % RAW, (m0 + (C_OFF + RAW)) * 4), m0 + (j - CH + 1))
                    else:
                        hi_run(m0)
                    if ups == 0:
                        act.wait_ge(sem("evacuated"), q * 8 + p * 2 + (G0 + 4 + e + 1))
                        for a in range(HALVES):
                            A(tmp[:, 2 * a:2 * a + 2, :].rearrange("p a b -> p (a b)"),
                              y[:, a, bass.ds(p * 1024 + e * GC, GC)], ACT.Square,
                              accum_out=ssq[:, a, bass.ds(p * 2 + e, 1)]).then_inc(sem("ysq"), 1)

                if last:
                    for p in range(2):
                        for e in range(2):
                            down(p, e, final=p == 1 and e == 1)
                else:
                    with act.Fori(0, 2) as p:
                        for e in range(2):
                            down(p, e)

            with act.Fori(0, QT) as q:
                mlp_quarter(G_ML1, 0, q)
            root(5)
            h_squares(4)
            root(6)
            act.wait_ge(sem("narrow_in"), 48)
            A(wsh[:, :, :], wsr[:, :, :], ACT.Copy).then_inc(sem("ws_hi"), 1)
            xt_hi(2, v("attn", KT))

            def lvl_exp(n):
                act.wait_ge(sem("lvl_d"), n + 1)
                A(eg[:, :, :], eg[:, :, :], ACT.Exp, scale=1.0 / GLA_TAU).then_inc(sem("lvl_e"), 1)

            def square(name, dst, src, ready, value=1):
                act.wait_ge(sem(ready), value)
                A(dst, src, ACT.Square).then_inc(sem(name + "_sq"), 1)

            def head_root(name, dst, b0, banks):
                act.wait_ge(sem(name + "_mm"), 1)
                A(flat(dst[:, :, :]).rearrange("p (b n) -> p b n", b=banks), ps[:, b0:b0 + banks, :], ACT.Sqrt,
                  bias=eps[:, 0:1], scale=1.0 / P).then_inc(sem(name + "_root"), 1)

            def soft_exp(name, pr):
                act.wait_ge(sem(name + "_max"), 1)
                for j in range(8):
                    A(pr[:, j, :], pr[:, j, :], ACT.Exp, bias=nmx[:, j:j + 1],
                      accum_out=sm[:, j:j + 1]).then_inc(sem(name + "_e"), 1)

            for k in range(len(WIN_GROUPS)):
                G = G_WIN + k
                hi_run(CH * G + 4)
                if k == 0:
                    act.wait_ge(sem("z_neg"), 2)
                    for t in (eg[:, :, :], fft[32:36, :]):
                        A(t, t, ACT.Exp).then_inc(sem("z_exp"), 1)
                    act.wait_ge(sem("z_exp"), 2)
                    for t in (eg[:, :, :], fft[32:36, :]):
                        A(t, t, ACT.Ln, bias=1.0).then_inc(sem("z_ln"), 1)
                if 2 <= k <= 5:
                    lvl_exp(2 * (k - 2) + 1)
                if k == 7:
                    head_root("o", osq, 4, 4)
                if k == 8:
                    soft_exp("fox", pf)
                if k == 9:
                    head_root("mq", tmp, 6, 2)
                    square("fo", fosq[:, :, :], ot[:, 8:12, :], "fo_out")
                if k == 10:
                    soft_exp("mem", pm)
                if k == 11:
                    square("mo", tmp[:, :, :], ot[:, 12:16, :], "mo_out")
                    head_root("mo", tmp, 6, 2)
                if k >= 8:
                    act.wait_ge(sem("chunk_used"), CH * G + CH)
                    b0 = 2 * (G % 2)
                    A(flat(gt[:, :, :]).rearrange("p (b n) -> p b n", b=2), ps[:, b0:b0 + 2, :], ACT.Exp,
                      scale=-1.0).then_inc(sem("gate_e"), 1)
                    act.wait_ge(sem("z_ready"), k - 7)
                    A(u[:, 4 * (k - 8):4 * (k - 7), 0, :], gt[:, :, :], ACT.Copy).then_inc(sem("z_hi"), 1)
                if 1 <= k <= 4:
                    lvl_exp(2 * (k - 1))
                if k == 6:
                    square("o", osq[:, :, :], ot[:, 0:8, :], "gla_out")
                    square("fq", fqsq[:, :, :], fq[:, :, :], "evacuated", G_WIN + 5)
                    square("fk", fksq[:, :, :], fk[:, :, :], "evacuated", G_WIN + 6)
                if k == 7:
                    square("mq", tmp[:, :, :], mq[:, :, :], "evacuated", G_WIN + 8)
                    head_root("fq", fqsq, 4, 2)
                    head_root("fk", fksq, 6, 2)
                if k == 9:
                    head_root("fo", fosq, 4, 2)
            for g in range(GQ):
                hi_run(CH * (G_WO + g) + 4)
                act.wait_ge(sem("evacuated"), G_WO + g + 1)
                for a in range(HALVES):
                    A(tmp[:, 2 * a:2 * a + 2, :].rearrange("p a b -> p (a b)"), h[:, a, g * GC:(g + 1) * GC], ACT.Square,
                      accum_out=ssq[:, a, g:g + 1]).then_inc(sem("osqs"), 1)
            root(7)
            xt_hi(3, v("mlp", KT))
            with act.Fori(0, QT - 1) as q:
                mlp_quarter(G_ML2, 4 * QT, q)
            mlp_quarter(G_ML2, 4 * QT, QT - 1, last=True)

        @block.vector
        def _(dve):
            V = nc.vector
            steps = [0]

            def link(ins):
                steps[0] += 1
                ins.then_inc(sem("dve_step"), 1)
                dve.wait_ge(sem("dve_step"), steps[0])

            def lo(i, s, hi_value):
                dve.wait_ge(sem("w_hi"), hi_value)
                V.tensor_tensor(flat(wl[:, i, :, :]), raw[:, s, :], flat(wh[:, i, :, :]).bitcast(F32),
                                ALU.subtract).then_inc(sem("raw_used"), 1)

            def lo_static(m):
                lo(m % CH, chunk_c(m) % RAW, m + 1)

            def lo_run(m0):
                for j in range(CH):
                    lo((4 + j) % CH, j % RAW, m0 + (j + 1))

            def gemv(cc, n, a):
                kt, half = divmod(n, 2)
                dve.wait_ge(sem(f"raw_landed{cc % RAW}"), 16 * (cc // RAW + 1))
                if cc >= 2:
                    dve.wait_ge(sem("raw_used"), cc - 1)
                t = acc[a][:, half * MODC:(half + 1) * MODC]
                V.scalar_tensor_tensor(out=t, in0=raw[:, cc % RAW, :], scalar=siluc[:, kt:kt + 1], in1=t,
                                       op0=ALU.mult, op1=ALU.add).then_inc(sem("raw_used"), 1)

            def mean(parts, n, done, value):
                dve.wait_ge(sem(done), value)
                V.tensor_reduce(ssm[:, :], ssq[:, :, 0:parts], AX.X, ALU.add).then_inc(sem("ssm_ready"), 1)
                dve.wait_ge(sem("rooted"), n)
                V.reciprocal(rstd[:, :], srt[:, :]).then_inc(sem("rs_ready"), 1)
                dve.wait_ge(sem("rs_ready"), n)

            def normed(src, name):
                for a in range(HALVES):
                    V.tensor_scalar(y[:, a, :], src[:, a, :], rstd[:, a:a + 1], None, ALU.mult).then_inc(sem(name), 1)

            def xt_lo_round(build, r, gain, shift=None):
                dve.wait_ge(sem("xt_hi"), 4 * build + r + 1)
                for j in range(4):
                    kt = 4 * r + j
                    src = ps[:, 4 + 2 * (r % 2) + j // 2, (j % 2) * S:(j % 2 + 1) * S]
                    if shift is None:
                        last = V.scalar_tensor_tensor(out=xt[:, kt, 1, :], in0=src, scalar=gain[:, kt:kt + 1],
                                                      in1=xt[:, kt, 0, :].bitcast(F32), op0=ALU.mult, op1=ALU.subtract)
                    else:
                        last = V.tensor_scalar(tmp[:, j, :], src, gain[:, kt:kt + 1], shift[:, kt:kt + 1], ALU.mult, ALU.add)
                if shift is not None:
                    link(last)
                    last = V.tensor_tensor(xt[:, 4 * r:4 * r + 4, 1, :], tmp[:, :, :],
                                           xt[:, 4 * r:4 * r + 4, 0, :].bitcast(F32), ALU.subtract)
                last.then_inc(sem("xt_ready"), 1)
                if shift is not None:
                    dve.wait_ge(sem("xt_ready"), 4 * build + r + 1)

            def mod_vector(n, dst, bank=7):
                dve.wait_ge(sem("mod_mm"), n)
                V.tensor_copy(dst, ps[:, bank, 0:KT]).then_inc(sem("mod_out"), 1)
                dve.wait_ge(sem("mod_out"), n)

            dve.wait_ge(sem("vt_mm"), 1)
            link(V.tensor_copy(vt[:, :], ps[:, 0, 0:VROWS]))
            link(V.tensor_scalar(v("fqg"), v("fqg"), float(P) ** -0.5, None, ALU.mult))
            V.tensor_scalar(v("mqg"), v("mqg"), float(P) ** -0.5, None, ALU.mult).then_inc(sem("vt_ready"), 1)
            V.tensor_copy(flat(lmask[:, :, :]), lmask_raw[:, :])
            dve.wait_ge(sem("c_exp"), 1)
            link(V.tensor_scalar(vtmp[:, :], vtmp[:, :], 1.0, None, ALU.add))
            link(V.reciprocal(vtmp[:, :], vtmp[:, :]))
            link(V.tensor_tensor(siluc[:, :], v("c", KT), vtmp[:, :], ALU.mult))
            mean(1, 1, "sq", 2)
            normed(y, "mem_normed")
            dve.wait_ge(sem("acc0_seeded"), 16)
            for n in range(MODN):
                if n % 4 == 3 and n < 16:
                    xt_lo_round(0, n // 4, v("mem", KT))
                if n == 16:
                    mean(1, 2, "sq", 4)
                if n == 20:
                    dve.wait_ge(sem("dft_hi"), 1)
                    V.tensor_tensor(dftl[:, :, :], dft_raw[:, :, :], dfth[:, :, :].bitcast(F32),
                                    ALU.subtract).then_inc(sem("dft_lo"), 1)
                if n in (24, 28):
                    a = (n - 24) // 4
                    dve.wait_ge(sem("xn_hi"), a + 1)
                    V.scalar_tensor_tensor(out=xn[:, 1, a, :], in0=h[:, a, :], scalar=rstd[:, a:a + 1],
                                           in1=xn[:, 0, a, :].bitcast(F32), op0=ALU.mult,
                                           op1=ALU.subtract).then_inc(sem("xn_lo"), 1)
                gemv(C_SC1 + n, n, 0)
            dve.wait_ge(sem("acc1_seeded"), 16)
            for m in range(2 * CH):
                lo_static(m)
                for j in range(2):
                    gemv(chunk_c(m) + 1 + j, 2 * m + j, 1)
                if m == 2:
                    mod_vector(1, vtmp[:, :])
                    link(V.tensor_scalar(vtmp[:, :], vtmp[:, :], 1.0, None, ALU.add))
                    link(V.tensor_tensor(a1[:, :], v("ng0", KT), vtmp[:, :], ALU.mult))
                    V.tensor_scalar(na1[:, :], a1[:, :], -1.0, None, ALU.mult).then_inc(sem("a1_ready"), 1)
                if m == CH + 3:
                    dve.wait_ge(sem("chunk_used"), CH)
                    V.tensor_copy(flat(mkt[:, :, :]).rearrange("p (b n) -> p b n", b=2), ps[:, 0:2, :]).then_inc(sem("evacuated"), 1)
            dve.wait_ge(sem("mk_root"), 1)
            link(V.reciprocal(mksq[:, :, :], mksq[:, :, :]))
            V.scalar_tensor_tensor(out=mkt[:, :, :], in0=mkt[:, :, :], scalar=v("mkg"), in1=mksq[:, :, :],
                                   op0=ALU.mult, op1=ALU.mult).then_inc(sem("mk_normed"), 1)
            dve.wait_ge(sem("chunk_used"), 2 * CH)
            V.tensor_copy(mvt[:, :, :], ps[:, 2:4, :]).then_inc(sem("evacuated"), 1)
            mod_vector(2, vtmp[:, :])
            V.tensor_scalar(s1[:, :], vtmp[:, :], float(S), None, ALU.mult).then_inc(sem("a1_ready"), 1)
            dve.wait_ge(sem("a1_ready"), 2)

            def p_lo(g):
                dve.wait_ge(sem("p_hi"), g + 1)
                for dt in range(2):
                    kt = 2 * g + dt
                    last = V.tensor_scalar(dc[:, dt:dt + 1], ps[:, 4 + 2 * (g % 2) + dt, 0:1], a1[:, kt:kt + 1],
                                           s1[:, kt:kt + 1], ALU.mult, ALU.add)
                last.then_inc(sem("dc_ready"), 1)
                for dt in range(2):
                    kt = 2 * g + dt
                    for o, n, t in ((1, S, a1), (S, 2 * S, na1)):
                        V.scalar_tensor_tensor(out=pdft[:, g % 2, dt, 1, o:n], in0=ps[:, 4 + 2 * (g % 2) + dt, o:n],
                                               scalar=t[:, kt:kt + 1], in1=pdft[:, g % 2, dt, 0, o:n].bitcast(F32),
                                               op0=ALU.mult, op1=ALU.subtract)
                dve.wait_ge(sem("dc_hi"), g + 1)
                V.tensor_tensor(pdft[:, g % 2, :, 1, 0:1].rearrange("p a b -> p (a b)"), dc[:, :],
                                pdft[:, g % 2, :, 0, 0:1].rearrange("p a b -> p (a b)").bitcast(F32),
                                ALU.subtract).then_inc(sem("p_lo"), 1)

            def fm_lo(g):
                dve.wait_ge(sem("fm_hi"), g + 1)
                V.tensor_tensor(xt[:, 2 * g:2 * g + 2, 1, :], ps[:, g % 2, :].rearrange("p (a b) -> p a b", a=2),
                                xt[:, 2 * g:2 * g + 2, 0, :].bitcast(F32), ALU.subtract).then_inc(sem("fm_lo"), 1)

            dve.wait_ge(sem("acc0_seeded"), 32)
            p_lo(0)
            for g in range(8):
                for n in range(4 * g, 4 * g + 4):
                    gemv(C_SC2 + n, n, 0)
                if g < 7:
                    p_lo(g + 1)
                fm_lo(g)
            dve.wait_ge(sem("acc1_seeded"), 32)

            def y_block(G):
                dve.wait_ge(sem("chunk_used"), CH * (G + 1))
                b0 = 2 * (G % 2)
                V.tensor_copy(y[:, :, (G - G_FN) * GC:(G - G_FN + 1) * GC], ps[:, b0:b0 + 2, :]).then_inc(sem("evacuated"), 1)

            for g in range(GQ):
                G = G_FN + g
                for i in range(CH):
                    lo_static(CH * G + i)
                    gemv(chunk_c(CH * G + i) + 1, CH * g + i, 1)
                    if g and i == 3:
                        y_block(G - 1)
                    if g == 1 and i == 4:
                        mod_vector(3, vtmp[:, :])
                        link(V.tensor_scalar(vtmp[:, :], vtmp[:, :], 1.0, None, ALU.add))
                        V.tensor_tensor(a2[:, :], v("ng2", KT), vtmp[:, :], ALU.mult).then_inc(sem("a2_ready"), 1)
            y_block(G_FN + GQ - 1)

            def gate(k, a, slot0):
                dve.wait_ge(sem("gate_mm"), k + 1)
                for half in range(2):
                    dve.wait_ge(sem("slot_in"), 16 * (slot0 + half + 1))
                    t = acc[a][:, half * MODC:(half + 1) * MODC].rearrange("p (b n) -> p b n", b=2)
                    V.tensor_tensor(t, ps[:, 4 + 2 * half:6 + 2 * half, :],
                                    slot[:, :].rearrange("p (b n) -> p b n", b=2), ALU.mult).then_inc(sem("slot_used"), 1)
                dve.wait_ge(sem("slot_used"), slot0 + 2)

            def residual(n, a_gate):
                a, b = divmod(n, 2)
                cols = slice(b * 1024, (b + 1) * 1024)
                link(V.scalar_tensor_tensor(out=y[:, a, cols], in0=y[:, a, cols], scalar=rstd[:, a:a + 1],
                                            in1=acc[a_gate][:, cols], op0=ALU.mult, op1=ALU.mult))
                V.tensor_tensor(h[:, a, cols], h[:, a, cols], y[:, a, cols], ALU.add).then_inc(sem("h_piece"), 1)

            dve.wait_ge(sem("acc0_seeded"), 48)
            for n in range(MODN):
                gemv(C_SH2 + n, n, 0)
                if n == 3:
                    gate(0, 1, 0)
                if n == 5:
                    mean(4, 3, "sq", 12)
                if n in (8, 11, 14, 17):
                    residual((n - 8) // 3, 1)
                if n == 20:
                    mean(2, 4, "hsq", 4)
                if n == 22:
                    normed(h, "x_normed")
            mod_vector(4, s2[:, :], 0)
            V.tensor_copy(vtmp[:, :], s2[:, :]).then_inc(sem("a2_ready"), 1)
            for i in range(4):
                lo_static(CH * G_ML1 + i)
            for r in range(4):
                xt_lo_round(1, r, a2, s2)

            def mlp_quarter(G0, ups, q, side, last=False):
                def side_chunk(p, e, down):
                    n = q * 8 + p * 2 + (e + 4 * down)
                    dve.wait_ge(sem("slot_in"), n * 16 + 48)
                    dve.wait_ge(sem("slot_used"), n + 1)
                    t = acc[0][:, e * MODC:(e + 1) * MODC]
                    V.scalar_tensor_tensor(out=t, in0=slot[:, :], scalar=siluc[:, bass.ds(q * 4 + p + 2 * down, 1)], in1=t,
                                           op0=ALU.mult, op1=ALU.add).then_inc(sem("slot_used"), 1)

                with dve.Fori(0, 2) as p:
                    for e in range(2):
                        lo_run(q * 64 + p * 16 + (CH * (G0 + e) + 4))
                        if side:
                            side_chunk(p, e, 0)
                        n, b0 = q * 4 + p * 2 + (ups + e), 4 * ((G0 + e) % 2)
                        dve.wait_ge(sem("up_lo"), n + 1)
                        V.tensor_tensor(tmp[:, :, :], ps[:, b0:b0 + 4, 0:S], tmp[:, :, :], ALU.add).then_inc(sem("evacuated"), 1)
                        dve.wait_ge(sem("evacuated"), q * 8 + p * 2 + (G0 + e + 1))
                        V.scalar_tensor_tensor(out=tmp[:, :, :], in0=tmp[:, :, :], scalar=0.0, in1=tmp[:, :, :],
                                               op0=ALU.max, op1=ALU.mult).then_inc(sem("up_sq"), 1)
                        dve.wait_ge(sem("u_hi"), n + 1)
                        w = bass.ds(p * 8 + 4 * e, 4)
                        V.tensor_tensor(u[:, w, 1, :], tmp[:, :, :], u[:, w, 0, :].bitcast(F32),
                                        ALU.subtract).then_inc(sem("u_lo"), 1)

                def down(p, e, final=False):
                    m0 = q * 64 + p * 16 + (CH * (G0 + 4 + e) + 4)
                    if final:
                        for j in range(4):
                            lo(4 + j, j % RAW, m0 + (j + 1))
                    else:
                        lo_run(m0)
                    if side:
                        side_chunk(p, e, 1)
                    dve.wait_ge(sem("chunk_used"), q * 64 + p * 16 + CH * (G0 + 4 + e + 1))
                    b0 = 4 * ((G0 + e) % 2)
                    cols = bass.ds(p * 1024 + e * GC, GC)
                    V.tensor_tensor(y[:, :, cols], y[:, :, cols], ps[:, b0:b0 + 2, :], ALU.add).then_inc(sem("evacuated"), 1)

                if last:
                    for p in range(2):
                        for e in range(2):
                            down(p, e, final=p == 1 and e == 1)
                else:
                    with dve.Fori(0, 2) as p:
                        for e in range(2):
                            down(p, e)

            dve.wait_ge(sem("acc0_seeded"), 64)
            dve.wait_ge(sem("y_zero"), 1)
            with dve.Fori(0, QT) as q:
                mlp_quarter(G_ML1, 0, q, True)
            mean(4, 5, "ysq", 8 * QT)
            gate(1, 0, 2 + MODN)
            for n in range(4):
                residual(n, 0)
            mean(2, 6, "hsq", 8)
            normed(h, "x_normed")
            dve.wait_ge(sem("ws_hi"), 1)
            V.tensor_tensor(wsl[:, :, :], wsr[:, :, :], wsh[:, :, :].bitcast(F32), ALU.subtract).then_inc(sem("ws_lo"), 1)
            for r in range(4):
                xt_lo_round(2, r, v("attn", KT))

            def banks(t, n=2):
                return flat(t).rearrange("p (b n) -> p b n", b=n)

            def scale_heads(t, gains, root, tiles):
                link(V.reciprocal(root, root))
                for j in range(tiles):
                    last = V.scalar_tensor_tensor(out=t[:, j, :], in0=t[:, j, :], scalar=gains(j), in1=root[:, j, :],
                                                  op0=ALU.mult, op1=ALU.mult)
                return last

            def lvl_parts(t, n):
                b = flat(t[:, :, :]).rearrange("p (n two m) -> p n two m", two=2, m=LEVELS[n])
                return b[:, :, 0, :], b[:, :, 1, :]

            def lvl_pre(n):
                m = LEVELS[n]
                b1, b2 = lvl_parts(bg, n)
                ref = b1[:, :, m - 1:m].to_broadcast([P, 512 // m, m])
                eq, ek = (flat(eg[:, 2 * i:2 * i + 2, :]).rearrange("p (n m) -> p n m", m=m) for i in range(2))
                if n == 0:
                    V.tensor_copy(eq, b2)
                else:
                    V.tensor_tensor(eq, b2, ref, ALU.subtract)
                V.tensor_tensor(ek, ref, b1, ALU.subtract).then_inc(sem("lvl_d"), 1)
                dve.wait_ge(sem("lvl_e"), n + 1)
                V.tensor_tensor(lvl_parts(qd, n)[1], eq, lvl_parts(qg, n)[1], ALU.mult)
                V.tensor_tensor(lvl_parts(kd, n)[0], ek, lvl_parts(kg, n)[0], ALU.mult).then_inc(sem("lvl_ready"), 1)

            def lvl_post(n):
                dve.wait_ge(sem("lvl_mm"), n + 1)
                if n == 0:
                    V.tensor_copy(banks(soff[:, :, :]), ps[:, 4:6, :]).then_inc(sem("lvl_out"), 1)
                else:
                    V.copy_predicated(sd[:, :, :], lmask[:, n - 1:n, :].to_broadcast([P, 16, P]),
                                      ps[:, 4:8, :].rearrange("p b (t n) -> p (b t) n", t=4)).then_inc(sem("lvl_out"), 1)

            def soft(name, pr, masked):
                dve.wait_ge(sem(name + "_qk"), 1)
                src, dst = ps[:, 4:8, :], banks(pr[:, :, :], 4)
                if masked:
                    link(V.tensor_tensor(dst, src, flat(mask[:, :, :]).rearrange("p (o n) -> p o n", o=1)
                                         .to_broadcast([P, 4, 2 * S]), ALU.add))
                else:
                    link(V.tensor_copy(dst, src))
                link(V.tensor_reduce(mx[:, :], pr[:, :, :], AX.X, ALU.max))
                V.tensor_scalar(nmx[:, :], mx[:, :], -1.0, None, ALU.mult).then_inc(sem(name + "_max"), 1)
                dve.wait_ge(sem(name + "_e"), 8)
                link(V.reciprocal(rs[:, :], sm[:, :]))
                for j in range(8):
                    last = V.tensor_scalar(pr[:, j, :], pr[:, j, :], rs[:, j:j + 1], None, ALU.mult)
                last.then_inc(sem(name + "_p"), 1)

            dve.wait_ge(sem("narrow_mm"), 1)
            V.tensor_copy(gat[0:16, :], ps[0:16, 4, 0:S]).then_inc(sem("gat_ready"), 1)
            V.tensor_scalar(ffz[32:36, :], ps[32:36, 4, 0:S], foxb[32:36, 0:1], None, ALU.add).then_inc(sem("gat_ready"), 1)
            fvv = flat(fv[:, :, :]).rearrange("p (a n) -> p a n", a=HALVES)
            into = dict(gk=kg, fq=fq, fk=fk, mq=mq)
            for k, (name, off) in enumerate(WIN_GROUPS):
                G = G_WIN + k
                lo_run(CH * G + 4)
                if k == 0:
                    dve.wait_ge(sem("la_mm"), 1)
                    for j in range(4):
                        last = V.tensor_scalar(bg[:, j, :], ps[:, 4 + j // 2, (j % 2) * S:(j % 2 + 1) * S], v("gab", 1, j),
                                               None, ALU.add)
                    link(last)
                    dve.wait_ge(sem("gat_ready"), 2)
                    for z, t in ((bg[:, :, :], eg[:, :, :]), (ffz[32:36, :], fft[32:36, :])):
                        V.scalar_tensor_tensor(out=t, in0=z, scalar=-1.0, in1=z, op0=ALU.mult, op1=ALU.min).then_inc(sem("z_neg"), 1)
                if 2 <= k <= 5:
                    lvl_post(2 * (k - 2))
                    lvl_pre(2 * (k - 2) + 1)
                if k == 6:
                    lvl_post(8)
                if k == 7:
                    dve.wait_ge(sem("o_root"), 1)
                    link(scale_heads(ot, lambda j: v("out", 1, j), osq[:, :, :], 8))
                if k == 8:
                    soft("fox", pf, True)
                if k == 9:
                    dve.wait_ge(sem("fox_pv"), 1)
                    V.tensor_copy(banks(ot[:, 8:12, :]), ps[:, 4:6, :]).then_inc(sem("fo_out"), 1)
                    dve.wait_ge(sem("mq_root"), 1)
                    link(scale_heads(mq, lambda j: v("mqg"), tmp[:, :, :], 4))
                if k == 10:
                    soft("mem", pm, False)
                if k == 11:
                    dve.wait_ge(sem("mem_pv"), 1)
                    V.tensor_copy(banks(ot[:, 12:16, :]), ps[:, 4:6, :]).then_inc(sem("mo_out"), 1)
                    dve.wait_ge(sem("mo_root"), 1)
                    link(scale_heads(ot[:, 12:16, :], lambda j: v("out", 1, 12 + j), tmp[:, :, :], 4))
                dve.wait_ge(sem("chunk_used"), CH * G + CH)
                src = ps[:, 2 * (G % 2):2 * (G % 2) + 2, :]
                if name == "gq":
                    V.tensor_scalar(banks(qg[:, :, :]), src, float(64) ** -0.5, None, ALU.mult).then_inc(sem("evacuated"), 1)
                elif name in into:
                    if k == 4:
                        dve.wait_ge(sem("h_spilled"), 16)
                    V.tensor_copy(banks(into[name][:, :, :]), src).then_inc(sem("evacuated"), 1)
                elif name == "gv":
                    V.tensor_copy(gv[:, :, off:off + GC], src).then_inc(sem("evacuated"), 1)
                elif name == "fv":
                    V.tensor_copy(fvv, src).then_inc(sem("evacuated"), 1)
                else:
                    kg_ = k - 8
                    g2d = banks(gt[:, :, :])
                    dve.wait_ge(sem("gate_e"), kg_ + 1)
                    first = V.tensor_scalar(gt[:, :, :], gt[:, :, :], 1.0, None, ALU.add)
                    if name == "gg":
                        link(first)
                    else:
                        first.then_inc(sem("evacuated"), 1)
                        dve.wait_ge(sem("evacuated"), G + 1)
                    link(V.reciprocal(gt[:, :, :], gt[:, :, :]))
                    if name == "gg":
                        V.tensor_tensor(g2d, src, g2d, ALU.mult).then_inc(sem("evacuated"), 1)
                        dve.wait_ge(sem("evacuated"), G + 1)
                    V.tensor_tensor(gt[:, :, :], gt[:, :, :], ot[:, 4 * kg_:4 * kg_ + 4, :], ALU.mult).then_inc(sem("z_ready"), 1)
                    dve.wait_ge(sem("z_hi"), kg_ + 1)
                    V.tensor_tensor(u[:, 4 * kg_:4 * kg_ + 4, 1, :], gt[:, :, :], u[:, 4 * kg_:4 * kg_ + 4, 0, :].bitcast(F32),
                                    ALU.subtract).then_inc(sem("z_lo"), 1)
                if k == 0:
                    dve.wait_ge(sem("z_ln"), 2)
                    for z, t in ((bg[:, :, :], eg[:, :, :]), (ffz[32:36, :], fft[32:36, :])):
                        link(V.scalar_tensor_tensor(out=t, in0=z, scalar=0.0, in1=t, op0=ALU.min, op1=ALU.subtract))
                    for j in range(4):
                        for tb in range(HALVES):
                            r = slice(tb * P, (tb + 1) * P)
                            last = V.tensor_tensor_scan(bg[:, j, r], ones[:, :], eg[:, j, r], 0.0, ALU.mult, ALU.add)
                    link(last)
                    link(V.tensor_tensor_scan(fc[32:36, 0:P], ones[32:36, :], fft[32:36, 0:P], 0.0, ALU.mult, ALU.add))
                    V.tensor_tensor_scan(fc[32:36, P:S], ones[32:36, :], fft[32:36, P:S], fc[32:36, P - 1:P],
                                         ALU.mult, ALU.add).then_inc(sem("fc_ready"), 1)
                if k == 1:
                    dve.wait_ge(sem("gla_zero"), 3)
                    lvl_pre(0)
                if 2 <= k <= 5:
                    lvl_post(2 * (k - 2) + 1)
                    if k <= 4:
                        lvl_pre(2 * (k - 1))
                if k == 6:
                    dve.wait_ge(sem("gla_mm"), 1)
                    V.tensor_copy(banks(ot[:, 0:8, :], 4), ps[:, 4:8, :]).then_inc(sem("gla_out"), 1)
                if k == 7:
                    dve.wait_ge(sem("fq_root"), 1)
                    dve.wait_ge(sem("fk_root"), 1)
                    link(scale_heads(fq, lambda j: v("fqg"), fqsq[:, :, :], 4))
                    scale_heads(fk, lambda j: v("fkg"), fksq[:, :, :], 4).then_inc(sem("fox_qk_ready"), 1)
                if k == 8:
                    dve.wait_ge(sem("fox_turn"), 1)
                    V.tensor_copy(pt[:, :, :, :].rearrange("p h a s -> p h (a s)"), ps[:, 4:8, :]).then_inc(sem("fox_pt"), 1)
                if k == 9:
                    dve.wait_ge(sem("fo_root"), 1)
                    last = scale_heads(ot[:, 8:12, :], lambda j: v("out", 1, 8 + j), fosq[:, :, :], 4)
                    last.then_inc(sem("mem_qk_ready"), 1)
                    dve.wait_ge(sem("mem_qk_ready"), 1)
                if k == 10:
                    dve.wait_ge(sem("mem_turn"), 1)
                    V.tensor_copy(pt[:, :, :, :].rearrange("p h a s -> p h (a s)"), ps[:, 4:8, :]).then_inc(sem("mem_pt"), 1)

            for g in range(GQ):
                G = G_WO + g
                lo_run(CH * G + 4)
                dve.wait_ge(sem("chunk_used"), CH * (G + 1))
                if g == 0:
                    dve.wait_ge(sem("h_back"), 16)
                cols = slice(g * GC, (g + 1) * GC)
                V.tensor_tensor(h[:, :, cols], h[:, :, cols], ps[:, 2 * (G % 2):2 * (G % 2) + 2, :],
                                ALU.add).then_inc(sem("evacuated"), 1)
            mean(4, 7, "osqs", 8)
            normed(h, "x_normed")
            for r in range(4):
                xt_lo_round(3, r, v("mlp", KT))
            dve.wait_ge(sem("y_zero"), 2)
            with dve.Fori(0, QT - 1) as q:
                mlp_quarter(G_ML2, 4 * QT, q, False)
            mlp_quarter(G_ML2, 4 * QT, QT - 1, False, last=True)
            dve.wait_ge(sem("evacuated"), G_ML2 + 2 * QT * GQ)
            for n in range(4):
                a, b = divmod(n, 2)
                cols = slice(b * 1024, (b + 1) * 1024)
                V.tensor_tensor(h[:, a, cols], h[:, a, cols], y[:, a, cols], ALU.add).then_inc(sem("out_ready"), 1)


WIN_GROUPS = [("gq", 0), ("gk", 0), ("gv", 0), ("gv", GC), ("fq", 0), ("fk", 0), ("fv", 0), ("mq", 0),
              ("gg", 0), ("gg", GC), ("fg", 0), ("mg", 0)]
N_CONSTS = 17

_INS = ["x", "c", "w_mod", "b_mod", "norm_g", "w_mlp_in", "w_mlp_out", "fnet_w_out", "mem_2", "attn_norm_g_2", "w_in_2",
        "gla_a_w2_2", "gla_a_b_2", "fox_f_b_2", "fox_q_norm_g_2", "fox_k_norm_g_2", "mem_norm_g_2", "w_mem_kv_2",
        "mem_q_norm_g_2", "mem_k_norm_g_2", "out_norm_g_2", "w_out_2", "mlp_norm_g_2", "w_up_2", "w_down_2"]


def shape_constants():
    n = np.arange(S)
    angle = 2 * np.pi * (np.outer(n, n) % S) / S
    i = np.arange(P)
    masks = [((i[None, :] // (2 * m) == i[:, None] // (2 * m)) & (i[None, :] % (2 * m) >= m) & (i[:, None] % (2 * m) < m))
             if m else i[None, :] == i[:, None] for m in LEVELS[1:]]
    keys = np.arange(S)
    causal = [np.where(keys[None, :] <= (tb * P + i)[:, None], 0.0, NEG) for tb in range(HALVES)]
    return {
        "k_ident": np.eye(P, dtype=np.float32),
        "k_dft": np.concatenate([np.cos(angle), np.sin(angle)], 1).astype(np.float32),
        "k_mask": np.concatenate(causal, 1).astype(np.float32),
        "k_nsel": np.repeat(-np.eye(4, dtype=np.float32), P, axis=1),
        "k_sel": np.eye(4, dtype=np.float32),
        "k_levels": np.concatenate(masks, 1).astype(np.float32),
    }


def kernel(**inputs):
    import numpy as _np
    import concourse.bacc as _bacc
    from concourse import mybir as _mybir
    from concourse.bass_utils import run_bass_kernel_spmd as _run

    nc = _bacc.Bacc("TRN2", target_bir_lowering=False, num_devices=1)
    arrays, args = {}, []
    for name, a in [(n, inputs[n]) for n in _INS] + list(shape_constants().items()):
        a = _np.ascontiguousarray(a)
        arrays[f"in_{name}_dram"] = a
        args.append(nc.dram_tensor(f"in_{name}_dram", a.shape, _mybir.dt.from_np(a.dtype), kind="ExternalInput").ap())
    args.append(nc.dram_tensor("out_0_dram", (1, S, D), F32, kind="ExternalOutput").ap())
    program(nc, *args)
    r = _run(nc, [arrays], core_ids=[0])
    return r.results[0]["out_0_dram"]
```

```python
from contextlib import ExitStack

import concourse.bass as bass
import numpy as np
from concourse import mybir

F32 = mybir.dt.float32
F32R = mybir.dt.float32r
U8 = mybir.dt.uint8
ALU = mybir.AluOpType
ACT = mybir.ActivationFunctionType
AX = mybir.AxisListType

P = 128
D = 2048
S = 256
HALVES = S // P
KT = D // P
FF = 4 * D
GC = 512
CH = 8
RAW = 4
QT = FF // D
GQ = D // GC
MODC = 1024
MODN = KT * D // MODC
PE_MOD = dict(sc1=(2, 8, 13, 18, 24), sh1=(), sc2=(), sh2=(3, 5, 20, 25))
EPS = 1e-6
NEG = -1e30
GLA_TAU = 16.0
LEVELS = (128, 64, 32, 16, 8, 4, 2, 1, 0)

W_IN = dict(gq=0, gk=512, gv=1024, gg=2048, ga=3072, fq=3088, fk=3600, fv=4112, fg=4624, ff=5136, mq=5140, mg=5652)
VROW = dict(c=0, ng0=16, ng2=32, attn=48, mem=64, mlp=80, out=96, gab=112, fqg=116, fkg=117, mqg=118, mkg=119)
VROWS = 120


def program(nc, x, c, w_mod, b_mod, norm_g, w_mlp_in, w_mlp_out, fnet_w_out, mem, attn_g, w_in, gla_w2, gla_b,
            fox_b, fox_qg, fox_kg, mem_g, w_mem_kv, mem_qg, mem_kg, out_g, w_out, mlp_g, w_up, w_down,
            k_ident, k_dft, k_mask, k_nsel, k_sel, k_levels, out):
    ctx = ExitStack()
    with ctx:
        sems = {}

        def sem(name):
            if name not in sems:
                sems[name] = ctx.enter_context(nc.semaphore(name))
            return sems[name]

        BASE = 16512
        KB = 1024
        O_RAW, O_WH, O_WL = 0, 16 * KB, 48 * KB
        O_H, O_XT, O_U, O_Y = 80 * KB, 96 * KB, 128 * KB, 160 * KB
        O_ACC0, O_ACC1, O_TMP, O_SLOT = 176 * KB, 184 * KB, 192 * KB, 196 * KB
        O_CONST = 200 * KB
        const_at = [O_CONST]

        def at(name, shape, dt, offset):
            return nc.alloc_sbuf_tensor_at(name, shape, dt, offset=BASE + offset)

        def const(name, shape, dt, size=4):
            n = int(np.prod(shape[1:])) * size
            t = at(name, shape, dt, const_at[0])
            const_at[0] += (n + 31) // 32 * 32
            assert const_at[0] <= 207 * KB + 800
            return t

        raw = at("raw", [P, RAW, MODC], F32, O_RAW)
        wh = at("wh", [P, CH, 2, GC], F32R, O_WH)
        wl = at("wl", [P, CH, 2, GC], F32R, O_WL)
        h = at("h", [P, HALVES, D], F32, O_H)
        xt = at("xt", [P, KT, 2, S], F32R, O_XT)
        u = at("u", [P, KT, 2, S], F32R, O_U)
        y = at("y", [P, HALVES, D], F32, O_Y)
        acc = [at(f"acc{i}", [P, D], F32, o) for i, o in enumerate((O_ACC0, O_ACC1))]
        tmp = at("tmp", [P, 4, S], F32, O_TMP)
        slot = at("slot", [P, MODC], F32, O_SLOT)
        xn = at("xn", [P, 2, HALVES, D], F32R, O_U)
        junk = at("junk", [P, D], F32, O_U)
        acc2 = at("acc2", [P, D], F32, O_U + 16 * KB)
        x1t = at("x1t", [P, KT, S], F32, O_U)
        mkt = at("mkt", [P, 4, S], F32, O_Y)
        mksq = at("mksq", [P, 4, S], F32, O_Y + 4 * KB)
        mvt = at("mvt", [P, HALVES, GC], F32, O_Y + 8 * KB)
        pdft = at("pdft", [P, 2, 2, 2, 2 * S], F32R, O_Y)
        dft_raw = at("dft_raw", [P, 2, 2 * S], F32, O_ACC1)
        lmask_raw = at("lmask_raw", [P, 8 * P], F32, O_ACC1 + 4 * KB)
        dfth = at("dfth", [P, 2, 2 * S], F32R, O_TMP)
        dftl = at("dftl", [P, 2, 2 * S], F32R, O_SLOT)
        AU = O_U
        qg, kg, bg, eg, qd, kd, soff = (at(n, [P, 4, S], F32, AU + i * 4 * KB)
                                        for i, n in enumerate(("qg", "kg", "bg", "eg", "qd", "kd", "soff")))
        gat, ffz, fft, fc = (at(n, [64, S], F32, AU + (28 + i) * KB) for i, n in enumerate(("gat", "ffz", "fft", "fc")))
        wsh = at("wsh", [P, KT, 64], F32R, AU + 16 * KB)
        wsl = at("wsl", [P, KT, 64], F32R, AU + 20 * KB)
        osq = at("osq", [P, 8, S], F32, AU)
        fqsq, fksq = (at(n, [P, 4, S], F32, AU + o * KB) for n, o in (("fqsq", 8), ("fksq", 12)))
        pf = at("pf", [P, 8, S], F32, AU + 16 * KB)
        fosq = at("fosq", [P, 4, S], F32, AU + 16 * KB)
        pm = at("pm", [P, 8, S], F32, AU + 24 * KB)
        fq, fk, fv, mq = (at(n, [P, 4, S], F32, O_H + i * 4 * KB) for i, n in enumerate(("fq", "fk", "fv", "mq")))
        pt = at("pt", [P, 4, 2, S], F32, O_H)
        ot = at("ot", [P, KT, S], F32, O_Y)
        sd = at("sd", [P, 16, P], F32, O_Y + 8 * KB)
        gv = at("gv", [P, HALVES, 2 * GC], F32, O_ACC0)
        gt = at("gt", [P, 4, S], F32, O_ACC0)
        wsr = at("wsr", [P, KT, 64], F32, O_ACC1)
        w2 = at("w2", [16, GC], F32, O_ACC1 + 4 * KB)
        mk = at("mk", [P, 4, S], F32, O_ACC1)
        mv = at("mv", [P, HALVES, GC], F32, O_ACC1 + 4 * KB)
        mask = at("mask", [P, HALVES, S], F32, O_SLOT)
        nsel = at("nsel", [64, 4, P], F32, O_SLOT + 2 * KB)
        ident = const("ident", [P, P], F32)
        ones = const("ones", [P, P], F32)
        vrow = const("vrow", [P, P], F32)
        vt = const("vt", [P, VROWS], F32)
        lmask = const("lmask", [P, 8, P], U8, 1)
        sel = const("sel", [64, 4], F32)
        foxb = const("foxb", [64, 1], F32)
        eps = const("eps", [P, 1], F32)
        siluc, a1, na1, s1, a2, s2, vtmp = (const(n, [P, KT], F32)
                                            for n in ("siluc", "a1", "na1", "s1", "a2", "s2", "vtmp"))
        ssq = const("ssq", [P, HALVES, 4], F32)
        ssm, srt, rstd = (const(n, [P, HALVES], F32) for n in ("ssm", "srt", "rstd"))
        dg = const("dg", [P, HALVES, P], F32)
        dc = const("dc", [P, 2], F32)
        mx, nmx, sm, rs = (const(n, [P, 8], F32) for n in ("mx", "nmx", "sm", "rs"))
        ps = ctx.enter_context(nc.psum_tensor("ps", [P, 8, 512], F32))
        mk_dram = nc.dram_tensor("mk_spill", [P, 4 * S], F32).ap()
        mv_dram = nc.dram_tensor("mv_spill", [P, HALVES * GC], F32).ap()
        h_dram = nc.dram_tensor("h_spill", [P, HALVES * D], F32).ap()

        def rows(w):
            return w.rearrange("(kt p) n -> p kt n", p=P)

        def flat(ap):
            return ap.rearrange("p a b -> p (a b)")

        def v(name, n=1, i=0):
            return vt[:, VROW[name] + i:VROW[name] + i + n]

        C_SC1 = 0
        C_MEM = C_SC1 + MODN
        C_G1 = C_MEM + 2 * CH + MODN
        C_FN = C_G1 + MODN
        C_SH2 = C_FN + GQ * CH + MODN
        C_ML1 = C_SH2 + MODN
        G_MEM, G_FN, G_ML1 = 0, 2, 2 + GQ
        G_WIN = G_ML1 + 2 * QT * GQ
        G_WO = G_WIN + 12
        G_ML2 = G_WO + GQ
        C_OFF = C_ML1 - CH * G_ML1

        def chunk_c(m):
            if m < CH * G_FN:
                return C_MEM + 3 * m
            if m < CH * G_ML1:
                return C_FN + 2 * (m - CH * G_FN)
            return m + C_OFF

        def slot_of(cc):
            return cc % RAW, cc // RAW + 1

        def mod_part(vec, n):
            return (n % KT, n // KT) if vec == "sh2" else divmod(n, 2)

        def mod_c(c0, n):
            if c0 == C_MEM:
                return C_MEM + 3 * (n // 2) + 1 + n % 2
            return C_FN + 2 * n + 1 if c0 == C_FN else c0 + n

        def row_loads(engine, part):
            vec_rows = [("c", c[0], KT), ("ng0", norm_g[0, 0], KT), ("ng2", norm_g[0, 2], KT), ("attn", attn_g, KT),
                        ("mem", mem_g, KT), ("mlp", mlp_g, KT), ("out", out_g, KT), ("gab", gla_b, 4),
                        ("fqg", fox_qg, 1), ("fkg", fox_kg, 1), ("mqg", mem_qg, 1), ("mkg", mem_kg, 1)]
            rows_of = [(ident[:, :], k_ident)] + [(vrow[VROW[n]:VROW[n] + k, :], t.rearrange("(a p) -> a p", p=P))
                                                  for n, t, k in vec_rows]
            assert len(rows_of) == N_ROWS
            for dst, src in rows_of[part::2]:
                engine.dma_start(dst, src).then_inc(sem(f"rows_in{part}"), 16)

        block = ctx.enter_context(nc.Block())

        @block.sync
        def _(sp):
            def load(cc, view):
                s = cc % RAW
                if cc >= RAW:
                    sp.wait_ge(sem(f"raw_used{s}"), cc // RAW)
                sp.dma_start(raw_slot(s, view), view).then_inc(sem(f"raw_landed{s}"), 16)

            def raw_slot(s, view):
                return raw[:, s, :] if len(view.shape) == 2 else raw[:, s, :].rearrange("p (t n) -> p t n", t=2)

            def mod_view(vec, n):
                kt, half = divmod(n, 2)
                return w_mod[0, kt * P:(kt + 1) * P, vec * D + half * MODC:vec * D + (half + 1) * MODC]

            def weight(w, i, col):
                return rows(w)[:, 2 * i:2 * i + 2, col:col + GC]

            sp.dma_start(y[:, :, :], mem[0].rearrange("(a p) d -> p a d", p=P)).then_inc(sem("mem_in"), 16)
            row_loads(sp, 1)
            for n in range(MODN):
                if n == RAW:
                    sp.dma_start(h[:, :, :], x[0].rearrange("(a p) d -> p a d", p=P)).then_inc(sem("x_in"), 16)
                load(C_SC1 + n, mod_view(1, n))
            for m in range(2 * CH):
                load(chunk_c(m), weight(w_mem_kv, m % CH, (m // CH) * GC))
                for j in range(2):
                    load(chunk_c(m) + 1 + j, mod_view(0, 2 * m + j))
            for n in range(MODN):
                load(C_G1 + n, mod_view(2, n))
            for m in range(CH * G_FN, CH * G_ML1):
                n = m - CH * G_FN
                load(chunk_c(m), weight(fnet_w_out[0], n % CH, (n // CH) * GC))
                load(chunk_c(m) + 1, mod_view(4, n))
            for n in range(MODN):
                load(C_SH2 + n, mod_view(3, 2 * (n % KT) + n // KT))

            def ring_group(r0, view_of):
                for i in range(CH):
                    sp.wait_ge(sem(f"raw_used{i % RAW}"), r0 + i // RAW)
                    sp.dma_start(raw[:, i % RAW, :].rearrange("p (t n) -> p t n", t=2),
                                 view_of(i)).then_inc(sem(f"raw_landed{i % RAW}"), 16)

            def mlp_loads(G0, w1, w2_):
                r0 = (CH * G0 + C_OFF) // RAW
                with sp.Fori(0, QT) as q:
                    with sp.Fori(0, GQ) as g:
                        ring_group(r0 + 16 * q + 2 * g,
                                   lambda i: rows(w1)[:, 2 * i:2 * i + 2, bass.ds(q * D + g * GC, GC)])
                    with sp.Fori(0, GQ) as g:
                        ring_group(r0 + 8 + 16 * q + 2 * g,
                                   lambda i: rows(w2_)[:, bass.ds(q * KT + 2 * i, 2), bass.ds(g * GC, GC)])

            mlp_loads(G_ML1, w_mlp_in[0], w_mlp_out[0])
            for k, (name, off) in enumerate(WIN_GROUPS):
                ring_group((CH * (G_WIN + k) + C_OFF) // RAW,
                           lambda i: rows(w_in)[:, 2 * i:2 * i + 2, W_IN[name] + off:W_IN[name] + off + GC])
            with sp.Fori(0, GQ) as g:
                ring_group((CH * G_WO + C_OFF) // RAW + 2 * g,
                           lambda i: rows(w_out)[:, 2 * i:2 * i + 2, bass.ds(g * GC, GC)])
            mlp_loads(G_ML2, w_up, w_down)
            for g in range(GQ):
                sp.wait_ge(sem("evacuated"), G_ML2 + 2 * QT * GQ - GQ + g + 1)
                sp.dma_start(out[0].rearrange("(a p) d -> p a d", p=P)[:, :, g * GC:(g + 1) * GC],
                             h[:, :, g * GC:(g + 1) * GC]).then_inc(sem("stored"), 16)
            sp.wait_ge(sem("stored"), 16 * GQ)

        @block.gpsimd
        def _(pool):
            pool.memset(ones[:, :], 1.0).then_inc(sem("const_set"), 1)
            pool.memset(eps[:, :], EPS).then_inc(sem("const_set"), 1)

            def seed(n, a, vec):
                t = (acc[0], acc[1], acc2)[a]
                pool.memset(t[:, :], 0.0).then_inc(sem("acc_zero"), 1)
                pool.wait_ge(sem("acc_zero"), n)
                pool.dma_start(t[0:1, :], b_mod[0:1, vec * D:(vec + 1) * D]).then_inc(sem(f"acc{a}_seeded"), 16)

            def side_gain(k, row, half):
                pool.dma_start(slot[:, :], norm_g[0, row:row + 1, half * MODC:(half + 1) * MODC]
                               .to_broadcast([P, MODC])).then_inc(sem("slot_in"), 16)

            seed(1, 0, 1)
            pool.wait_ge(sem("dft_lo"), 1)
            seed(2, 1, 0)
            pool.wait_ge(sem("mod_out"), 1)
            seed(3, 0, 2)
            pool.wait_ge(sem("mod_out"), 2)
            seed(4, 1, 4)
            pool.wait_ge(sem("dft_d"), 8)
            side_gain(0, 1, 0)
            pool.wait_ge(sem("slot_used"), 1)
            side_gain(1, 1, 1)
            seed(5, 2, 3)
            pool.wait_ge(sem("evacuated"), G_ML1)
            seed(6, 0, 5)
            pool.wait_ge(sem("h_piece"), 4)
            pool.memset(y[:, :, :], 0.0).then_inc(sem("y_zero"), 1)
            with pool.Fori(0, QT * GQ) as n2:
                for half in range(2):
                    if half == 0:
                        pool.wait_ge(sem("slot_used"), n2 * 2 + 2)
                    else:
                        pool.wait_ge(sem("slot_used"), n2 * 2 + 3)
                    pool.dma_start(slot[:, :], rows(w_mod[0])[:, bass.ds(n2, 1), 5 * D + half * MODC:5 * D + (half + 1) * MODC]
                                   .rearrange("p a n -> p (a n)")).then_inc(sem("slot_in"), 16)
            pool.memset(wsr[:, :, :], 0.0).then_inc(sem("wsr_zero"), 1)
            pool.wait_ge(sem("wsr_zero"), 1)
            pool.dma_start(wsr[:, :, 0:16], rows(w_in)[:, :, W_IN["ga"]:W_IN["ga"] + 16]).then_inc(sem("narrow_in"), 16)
            pool.dma_start(wsr[:, :, 32:36], rows(w_in)[:, :, W_IN["ff"]:W_IN["ff"] + 4]).then_inc(sem("narrow_in"), 16)
            pool.dma_start(w2[:, :], gla_w2).then_inc(sem("narrow_in"), 16)
            for half in range(2):
                if half == 0:
                    pool.wait_ge(sem("slot_used"), 2 + MODN)
                else:
                    pool.wait_ge(sem("slot_used"), 3 + MODN)
                side_gain(2 + half, 3, half)
            pool.wait_ge(sem("slot_used"), 4 + MODN)
            pool.dma_start(mask[:, :, :], k_mask.rearrange("p (a s) -> p a s", a=HALVES)).then_inc(sem("att_const"), 16)
            pool.dma_start(nsel[32:36, :, :], k_nsel.rearrange("p (a s) -> p a s", a=4)).then_inc(sem("att_const"), 16)
            pool.wait_ge(sem("h_piece"), 8)
            pool.dma_start(h_dram, flat(h[:, :, :])).then_inc(sem("h_spilled"), 16)
            pool.wait_ge(sem("la_mm"), 1)
            for t in (qd, kd, sd):
                pool.memset(t[:, :, :], 0.0).then_inc(sem("gla_zero"), 1)
            pool.wait_ge(sem("mkv_spilled"), 32)
            pool.dma_start(flat(mk[:, :, :]), mk_dram).then_inc(sem("mkv_in"), 16)
            pool.dma_start(flat(mv[:, :, :]), mv_dram).then_inc(sem("mkv_in"), 16)
            pool.wait_ge(sem("mem_pv"), 1)
            pool.wait_ge(sem("h_spilled"), 16)
            pool.dma_start(flat(h[:, :, :]), h_dram).then_inc(sem("h_back"), 16)

        @block.tensor
        def _(pe):
            mm = nc.tensor.matmul

            def T_chunk(G, i, wide, s, r):
                pe.wait_ge(sem(f"raw_used{s}"), r)
                par = G % 2
                for t in range(2):
                    kt = 2 * i + t
                    for j in range(4):
                        a, b = wh[:, i, t, j * P:(j + 1) * P], wl[:, i, t, j * P:(j + 1) * P]
                        first, end = kt == 0, kt == KT - 1
                        if wide:
                            o = ps[:, 4 * par + j, :]
                            mm(o, a, flat(xt[:, kt, :, :]), start=first, stop=end, skip_group_check=True)
                            last = mm(o[:, 0:S], b, xt[:, kt, 0, :], start=False, stop=end, skip_group_check=True)
                        else:
                            o = ps[:, 2 * par + j // 2, (j % 2) * S:(j % 2 + 1) * S]
                            mm(o, a, xt[:, kt, 0, :], start=first and j % 2 == 0, stop=False, skip_group_check=True)
                            mm(o, a, xt[:, kt, 1, :], start=False, stop=False, skip_group_check=True)
                            last = mm(o, b, xt[:, kt, 0, :], start=False, stop=end, skip_group_check=True)
                last.then_inc(sem("chunk_used"), 1)

            def N_chunk(G, i, act, wide, s, r):
                pe.wait_ge(sem(f"raw_used{s}"), r)
                par = G % 2
                for t in range(2):
                    kt = 2 * i + t
                    for half in range(HALVES):
                        o = ps[:, (4 if wide else 2) * par + half, :]
                        hi, lo = (act[:, kt, z, half * P:(half + 1) * P] for z in range(2))
                        mm(o, hi, wh[:, i, t, :], start=kt == 0, stop=False, skip_group_check=True)
                        mm(o, hi, wl[:, i, t, :], start=False, stop=False, skip_group_check=True)
                        last = mm(o, lo, wh[:, i, t, :], start=False, stop=kt == KT - 1, skip_group_check=True)
                last.then_inc(sem("chunk_used"), 1)

            def bank_free(G):
                if not isinstance(G, int) or G >= 2:
                    pe.wait_ge(sem("evacuated"), G - 1)

            def transposes(build, src, rounds=range(4), drained=None):
                for half in range(HALVES):
                    pe.wait_ge(sem("dg_ready"), 2 * build + half + 1)
                for r in rounds:
                    if r >= 2:
                        if drained is None:
                            pe.wait_ge(sem("xt_ready"), 4 * build + r - 1)
                        else:
                            pe.wait_ge(sem(drained), r - 1)
                    for j in range(4):
                        for half in range(HALVES):
                            kt = 4 * r + j
                            last = mm(ps[:, 4 + 2 * (r % 2) + j // 2, (j % 2) * S + half * P:(j % 2) * S + (half + 1) * P],
                                      src[:, half, kt * P:(kt + 1) * P], dg[:, half, :], start=True, stop=True)
                    last.then_inc(sem("turned"), 1)

            for part in range(2):
                pe.wait_ge(sem(f"rows_in{part}"), 16 * ((N_ROWS + 1 - part) // 2))
            nc.tensor.transpose(ps[:, 0, 0:VROWS], vrow[0:VROWS, :], ident[0:VROWS, 0:VROWS]).then_inc(sem("vt_mm"), 1)

            def mod_chunk(vec, c0, n, bank, start=False):
                kt, half = mod_part(vec, n)
                s, r = slot_of(mod_c(c0, n))
                pe.wait_ge(sem(f"raw_landed{s}"), 16 * r)
                for j in range(8):
                    last = mm(ps[:, bank, 8 * half + j:8 * half + j + 1], raw[:, s, j * P:(j + 1) * P], siluc[:, kt:kt + 1],
                              start=start and j == 0, stop=False, skip_group_check=True)
                last.then_inc(sem(f"raw_used{s}"), 1)

            def mod_sum(vec, c0, a, bank, halves=(0, 1)):
                for half in halves:
                    n = [n for n in range(MODN) if mod_part(vec, n)[1] == half and n not in PE_MOD[vec]][-1]
                    s, r = slot_of(mod_c(c0, n))
                    pe.wait_ge(sem(f"raw_used{s}"), r)
                alone = not [n for n in PE_MOD[vec] if mod_part(vec, n)[1] in halves]
                for kt in range(8 * halves[0], 8 * halves[-1] + 8):
                    last = mm(ps[:, bank, kt:kt + 1], (acc[0], acc[1], acc2)[a][:, kt * P:(kt + 1) * P], ones[:, 0:1], start=alone, stop=True,
                              skip_group_check=True)
                last.then_inc(sem("mod_mm"), 1)

            pe.wait_ge(sem("silu_ready"), 1)
            for n in range(MODN):
                if n in (4, 6, 8, 10):
                    transposes(0, y, [(n - 4) // 2])
                if n in PE_MOD["sc1"]:
                    mod_chunk("sc1", C_SC1, n, 2, n == PE_MOD["sc1"][0])
            pe.wait_ge(sem("const_set"), 2)
            mod_sum("sc1", C_SC1, 0, 2)
            for i in range(CH):
                if i % 2 == 0:
                    pe.wait_ge(sem("xt_ready"), 1 + i // 2)
                T_chunk(G_MEM, i, False, *slot_of(chunk_c(i)))
            for i in range(CH):
                if i == 0:
                    pe.wait_ge(sem("mod_out"), 1)
                N_chunk(G_MEM + 1, i, xt, False, *slot_of(chunk_c(CH + i)))
                if i == 3:
                    pe.wait_ge(sem("mksq_ready"), 1)
                    for n in range(2):
                        last = mm(ps[:, 4 + n, :], ones[:, :], flat(mksq[:, 2 * n:2 * n + 2, :]), start=True, stop=True)
                    last.then_inc(sem("mk_mm"), 1)
            def dft_tokens(g):
                for dt in range(2):
                    if g >= 2:
                        pe.wait_ge(sem("p_lo"), g - 1)
                    o = ps[:, 4 + 2 * (g % 2) + dt, :]
                    d0 = (2 * g + dt) * P
                    for half in range(HALVES):
                        for z, t in ((0, dfth), (0, dftl), (1, dfth)):
                            last = mm(o, xn[:, z, half, d0:d0 + P], t[:, half, :], start=half == 0 and z == 0 and t is dfth,
                                      stop=half == 1 and z == 1, skip_group_check=True)
                last.then_inc(sem("dft_t"), 1)

            def dft_features(g):
                pe.wait_ge(sem("p_lo"), g + 1)
                if g >= 2:
                    pe.wait_ge(sem("fm_lo"), g - 1)
                for dq in range(2):
                    o = ps[:, g % 2, dq * S:(dq + 1) * S]
                    for kt in range(2):
                        for part in range(2):
                            lhs = slice(part * S + dq * P, part * S + (dq + 1) * P)
                            mv_ = slice(part * S, (part + 1) * S)
                            start = dq == 0 and kt == 0 and part == 0
                            mm(o, dfth[:, kt, lhs], pdft[:, g % 2, kt, 0, mv_], start=start, stop=False, skip_group_check=True)
                            mm(o, dftl[:, kt, lhs], pdft[:, g % 2, kt, 0, mv_], start=False, stop=False, skip_group_check=True)
                            last = mm(o, dfth[:, kt, lhs], pdft[:, g % 2, kt, 1, mv_], start=False,
                                      stop=kt == 1 and part == 1, skip_group_check=True)
                last.then_inc(sem("dft_d"), 1)

            pe.wait_ge(sem("xn_lo"), 2)
            pe.wait_ge(sem("dft_lo"), 1)
            pe.wait_ge(sem("mk_ln"), 1)
            dft_tokens(0)
            mod_sum("sh1", C_MEM, 1, 7)
            pe.wait_ge(sem("mod_out"), 2)
            pe.wait_ge(sem("evacuated"), 2)
            for g in range(8):
                if g < 7:
                    dft_tokens(g + 1)
                dft_features(g)

            def gate_rows(k, banks, a=0):
                for n, b in enumerate(banks):
                    last = mm(ps[:, b, :], ones[:, :], acc[a][:, n * GC:(n + 1) * GC], start=True, stop=True)
                last.then_inc(sem("gate_mm"), 1)

            for n in (MODN - 2, MODN - 1):
                s, r = slot_of(mod_c(C_G1, n))
                pe.wait_ge(sem(f"raw_used{s}"), r)
            gate_rows(0, (4, 5, 6, 7))

            for g in range(GQ):
                bank_free(G_FN + g)
                for i in range(CH):
                    if g == 0:
                        pe.wait_ge(sem("fm_lo"), i + 1)
                    N_chunk(G_FN + g, i, xt, False, *slot_of(chunk_c(CH * (G_FN + g) + i)))

            pe.wait_ge(sem("slot_used"), 2)
            mod_sum("sc2", C_FN, 1, 7)
            pe.wait_ge(sem("evacuated"), G_ML1 - 1)
            for n in range(MODN):
                if n == KT:
                    mod_sum("sh2", C_SH2, 2, 0, (0,))
                if n == SH2_TURN:
                    pe.wait_ge(sem("mod_out"), 3)
                    transposes(1, h, drained="x1t_out")
                    pe.wait_ge(sem("x1t_out"), 4)
                if n in PE_MOD["sh2"]:
                    mod_chunk("sh2", C_SH2, n, 7 * (n // KT), n in (PE_MOD["sh2"][0], min(m for m in PE_MOD["sh2"] if m >= KT)))
            mod_sum("sh2", C_SH2, 2, 7, (1,))

            def mlp(G0, build, ups, between=None):
                r0 = (CH * G0 + C_OFF) // RAW

                def down(q, p, e, last=False):
                    pe.wait_ge(sem("evacuated"), q * 8 + p * 2 + (G0 + 4 + e - 1))
                    for i in range(CH):
                        if i % 2 == 0 and e == 0:
                            pe.wait_ge(sem("u_lo"), q * 4 + (ups + i // 2 + 1))
                        N_chunk(G0 + e, i, u, True, i % RAW, q * 16 + p * 4 + (r0 + 8 + 2 * e + i // RAW + 1))
                        if last and i == 1:
                            between()

                def quarter(q, last=False):
                    with pe.Fori(0, 2) as p:
                        for e in range(2):
                            pe.wait_ge(sem("evacuated"), q * 8 + p * 2 + (G0 + e - 1))
                            for i in range(CH):
                                if i % 2 == 0 and e == 0:
                                    pe.wait_ge(sem("xt_ready"), 4 * build + 1 + i // 2)
                                T_chunk(G0 + e, i, True, i % RAW, q * 16 + p * 4 + (r0 + 2 * e + i // RAW + 1))
                    if last:
                        for p in range(2):
                            for e in range(2):
                                down(q, p, e, last=p == 1 and e == 1)
                    else:
                        with pe.Fori(0, 2) as p:
                            for e in range(2):
                                down(q, p, e)

                if between:
                    with pe.Fori(0, QT - 1) as q:
                        quarter(q)
                    quarter(QT - 1, last=True)
                else:
                    with pe.Fori(0, QT) as q:
                        quarter(q)

            def g2_rows():
                pe.wait_ge(sem("slot_used"), 2 + MODN)
                gate_rows(1, (2, 3, 6, 7))

            mlp(G_ML1, 1, 0, g2_rows)
            transposes(2, h)

            def att_narrow():
                pe.wait_ge(sem("ws_lo"), 1)
                pe.wait_ge(sem("xt_ready"), 12)
                for kt in range(KT):
                    for n, (w, z) in enumerate(((wsh, 0), (wsh, 1), (wsl, 0))):
                        last = mm(ps[0:64, 4, 0:S], w[:, kt, :], xt[:, kt, z, :], start=kt == 0 and n == 0,
                                  stop=kt == KT - 1 and n == 2, skip_group_check=True)
                last.then_inc(sem("narrow_mm"), 1)

            def att_la():
                pe.wait_ge(sem("gat_ready"), 2)
                for j in range(4):
                    last = mm(ps[:, 4 + j // 2, (j % 2) * S:(j % 2 + 1) * S], w2[:, j * P:(j + 1) * P], gat[0:16, :],
                              start=True, stop=True)
                last.then_inc(sem("la_mm"), 1)

            def att_level(n):
                diag = LEVELS[n] == 0
                if diag:
                    pe.wait_ge(sem("lvl_out"), n)
                else:
                    pe.wait_ge(sem("lvl_ready"), n + 1)
                ka, qa = (kg, qg) if diag else (kd, qd)
                for hd in range(8):
                    o64 = 64 * (hd % 2)
                    for tb in range(1 if n == 0 else HALVES):
                        col = (4 * (hd % 2) + hd // 2 if n == 0 else 8 * (hd % 2) + 2 * (hd // 2) + tb) * P
                        i0 = P if n == 0 else tb * P
                        last = mm(ps[:, 4 + col // 512, col % 512:col % 512 + P],
                                  ka[o64:o64 + 64, hd // 2, tb * P:(tb + 1) * P],
                                  qa[o64:o64 + 64, hd // 2, i0:i0 + P], start=True, stop=True)
                last.then_inc(sem("lvl_mm"), 1)

            def att_gla_out():
                pe.wait_ge(sem("lvl_out"), len(LEVELS))
                for hd in range(8):
                    o = ps[:, 4 + hd // 2, (hd % 2) * S:(hd % 2 + 1) * S]
                    v0, v1 = (gv[:, a, hd * P:(hd + 1) * P] for a in range(2))
                    at0, off = 8 * (hd % 2) + 2 * (hd // 2), (4 * (hd % 2) + hd // 2) * P
                    mm(o[:, 0:P], v0, sd[:, at0, :], start=hd % 2 == 0, stop=True, skip_group_check=True)
                    mm(o[:, P:S], v0, flat(soff[:, :, :])[:, off:off + P], start=False, stop=False, skip_group_check=True)
                    last = mm(o[:, P:S], v1, sd[:, at0 + 1, :], start=False, stop=True, skip_group_check=True)
                last.then_inc(sem("gla_mm"), 1)

            def att_sums(name, n, sq, tiles, bank):
                pe.wait_ge(sem(name + "_sq"), n)
                for j in range(tiles // 2):
                    last = mm(ps[:, bank + j, :], ones[:, :], flat(sq[:, 2 * j:2 * j + 2, :]), start=True, stop=True)
                last.then_inc(sem(name + "_mm"), 1)

            def att_qk(name, qq, kk, fox):
                pe.wait_ge(sem(name + "_qk_ready"), 1)
                for hd in range(4):
                    for tb in range(HALVES):
                        o = ps[:, 4 + hd, tb * S:(tb + 1) * S]
                        last = mm(o, qq[:, hd, tb * P:(tb + 1) * P], kk[:, hd, :], start=tb == 0, stop=not fox,
                                  skip_group_check=True)
                        if fox:
                            mm(o, fc[32:36, tb * P:(tb + 1) * P], sel[32:36, hd:hd + 1].to_broadcast([4, S]),
                               start=False, stop=False, skip_group_check=True)
                            last = mm(o, nsel[32:36, hd, :], fc[32:36, :], start=False, stop=True, skip_group_check=True)
                last.then_inc(sem(name + "_qk"), 1)

            def att_turn(name, pr):
                pe.wait_ge(sem(name + "_p"), 1)
                for hd in range(4):
                    for tb in range(HALVES):
                        for sb_ in range(HALVES):
                            last = nc.tensor.transpose(ps[:, 4 + hd, sb_ * S + tb * P:sb_ * S + (tb + 1) * P],
                                                       pr[:, 2 * hd + tb, sb_ * P:(sb_ + 1) * P], ident[:, :])
                last.then_inc(sem(name + "_turn"), 1)

            def att_pv(name, val):
                pe.wait_ge(sem(name + "_pt"), 1)
                for hd in range(4):
                    for sb_ in range(HALVES):
                        last = mm(ps[:, 4 + hd // 2, (hd % 2) * S:(hd % 2 + 1) * S], val(sb_, hd), pt[:, hd, sb_, :],
                                  start=sb_ == 0 and hd % 2 == 0, stop=sb_ == 1, skip_group_check=True)
                last.then_inc(sem(name + "_pv"), 1)

            fvv = flat(fv[:, :, :]).rearrange("p (a n) -> p a n", a=HALVES)
            for k, (name, off) in enumerate(WIN_GROUPS):
                G = G_WIN + k
                bank_free(G)
                for i in range(CH):
                    if k == 0 and i % 2 == 0:
                        pe.wait_ge(sem("xt_ready"), 8 + i // 2 + 1)
                    sr = slot_of(CH * G + C_OFF + i)
                    if name in ("gv", "fv"):
                        N_chunk(G, i, xt, False, *sr)
                    else:
                        T_chunk(G, i, False, *sr)
                    if (k, i) == (0, 1):
                        att_narrow()
                    if (k, i) == (0, 5):
                        att_la()
                    if 2 <= k <= 6 and i == 3:
                        att_level(2 * (k - 2))
                    if 2 <= k <= 5 and i == 6:
                        att_level(2 * (k - 2) + 1)
                    if (k, i) == (6, 6):
                        att_gla_out()
                    if (k, i) == (7, 3):
                        att_sums("o", 1, osq, 8, 4)
                    if (k, i) == (7, 7):
                        pe.wait_ge(sem("o_ln"), 1)
                        att_sums("fq", 1, fqsq, 4, 4)
                        att_sums("fk", 1, fksq, 4, 6)
                    if (k, i) == (8, 3):
                        pe.wait_ge(sem("att_const"), 32)
                        att_qk("fox", fq, fk, True)
                    if (k, i) == (9, 0):
                        att_turn("fox", pf)
                    if (k, i) == (9, 4):
                        att_pv("fox", lambda sb_, hd: fvv[:, sb_, hd * P:(hd + 1) * P])
                        att_sums("mq", 1, tmp, 4, 6)
                    if (k, i) == (9, 7):
                        att_sums("fo", 1, fosq, 4, 4)
                    if (k, i) == (10, 3):
                        pe.wait_ge(sem("mkv_in"), 32)
                        pe.wait_ge(sem("fo_ln"), 1)
                        att_qk("mem", mq, mk, False)
                    if (k, i) == (11, 2):
                        att_turn("mem", pm)
                    if (k, i) == (11, 5):
                        att_pv("mem", lambda sb_, hd: mv[:, sb_, hd * P:(hd + 1) * P])
                    if (k, i) == (11, 7):
                        att_sums("mo", 1, tmp, 4, 6)

            with pe.Fori(0, 2) as p:
                for e in range(2):
                    pe.wait_ge(sem("evacuated"), p * 2 + (G_WO + e - 1))
                    for i in range(CH):
                        if i % 2 == 0 and e == 0:
                            pe.wait_ge(sem("z_lo"), i // 2 + 1)
                        N_chunk(G_WO + e, i, u, False, i % RAW, p * 4 + ((CH * G_WO + C_OFF) // RAW + 2 * e + i // RAW + 1))
            transposes(3, h)
            mlp(G_ML2, 3, 16)

        @block.scalar
        def _(act):
            A = nc.scalar.activation
            col = lambda t: t.rearrange("(a o) -> a o", o=1)
            consts = [(dft_raw[:, :, :], k_dft.rearrange("(a p) n -> p a n", p=P)),
                      (foxb[32:36, :], col(fox_b)), (sel[32:36, :], k_sel), (lmask_raw[:, :], k_levels)]
            assert len(consts) == N_CONSTS
            row_loads(act, 0)
            for dst, src in consts:
                act.dma_start(dst, src).then_inc(sem("consts_in"), 16)

            def hi(i, landed, used):
                act.wait_ge(sem(f"raw_landed{landed[0]}"), landed[1])
                if used is not None:
                    act.wait_ge(sem("chunk_used"), used)
                A(flat(wh[:, i, :, :]), raw[:, landed[0], :], ACT.Copy).then_inc(sem("w_hi"), 1)

            def hi_static(m):
                cc = chunk_c(m)
                hi(m % CH, (cc % RAW, 16 * (cc // RAW + 1)), m - CH + 1 if m >= CH else None)

            def hi_run(m0, between=None):
                for j in range(CH):
                    if between and j < 4:
                        between(j)
                    i = (4 + j) % CH
                    hi(i, (j % RAW, (m0 + (C_OFF + RAW * (j // RAW) + RAW)) * 4), m0 + (j - CH + 1))

            def root(n):
                act.wait_ge(sem("ssm_ready"), n)
                A(srt[:, :], ssm[:, :], ACT.Sqrt, bias=eps[:, 0:1], scale=1.0 / D).then_inc(sem("rooted"), 1)

            def xt_hi(build, gain):
                for r in range(4):
                    act.wait_ge(sem("turned"), 4 * build + r + 1)
                    for j in range(4):
                        src = ps[:, 4 + 2 * (r % 2) + j // 2, (j % 2) * S:(j % 2 + 1) * S]
                        kt = 4 * r + j
                        last = A(xt[:, kt, 0, :], src, ACT.Copy, scale=gain[:, kt:kt + 1])
                    last.then_inc(sem("xt_hi"), 1)

            act.wait_ge(sem("vt_ready"), 1)
            A(vtmp[:, :], v("c", KT), ACT.Exp, scale=-1.0).then_inc(sem("c_exp"), 1)
            act.wait_ge(sem("mem_in"), 16)
            act.wait_ge(sem("const_set"), 2)
            for a in range(HALVES):
                A(junk[:, :], y[:, a, :], ACT.Square, accum_out=ssq[:, a, 0:1]).then_inc(sem("sq"), 1)
                act.wait_ge(sem("sq"), a + 1)
            root(1)
            act.wait_ge(sem("rs_ready"), 1)
            xt_hi(0, v("mem", KT))
            act.wait_ge(sem("x_in"), 16)
            for a in range(HALVES):
                A(junk[:, :], h[:, a, :], ACT.Square, accum_out=ssq[:, a, 0:1]).then_inc(sem("sq"), 1)
                act.wait_ge(sem("sq"), 3 + a)
            root(2)
            act.wait_ge(sem("consts_in"), 16 * N_CONSTS)
            A(dfth[:, :, :], dft_raw[:, :, :], ACT.Copy).then_inc(sem("dft_hi"), 1)
            act.wait_ge(sem("rs_ready"), 2)
            for a in range(HALVES):
                A(xn[:, 0, a, :], h[:, a, :], ACT.Copy, scale=rstd[:, a:a + 1]).then_inc(sem("xn_hi"), 1)
            for m in range(CH + 4):
                hi_static(m)
            act.wait_ge(sem("chunk_used"), CH)
            A(flat(mksq[:, :, :]).rearrange("p (b n) -> p b n", b=2), ps[:, 0:2, :], ACT.Square).then_inc(sem("mksq_ready"), 1)
            A(flat(mkt[:, :, :]).rearrange("p (b n) -> p b n", b=2), ps[:, 0:2, :], ACT.Copy).then_inc(sem("evacuated"), 1)
            for m in range(CH + 4, 2 * CH):
                hi_static(m)
            act.wait_ge(sem("mk_mm"), 1)
            A(flat(mksq[:, :, :]).rearrange("p (b n) -> p b n", b=2), ps[:, 4:6, :], ACT.Ln, bias=eps[:, 0:1],
              scale=1.0 / P).then_inc(sem("mk_ln"), 1)
            act.wait_ge(sem("mk_ln"), 1)
            A(mksq[:, :, :], mksq[:, :, :], ACT.Exp, scale=-0.5).then_inc(sem("mk_root"), 1)
            act.wait_ge(sem("chunk_used"), 2 * CH)
            A(mvt[:, :, :], ps[:, 2:4, :], ACT.Copy).then_inc(sem("evacuated"), 1)
            act.wait_ge(sem("mk_normed"), 1)
            act.dma_start(mk_dram, flat(mkt[:, :, :])).then_inc(sem("mkv_spilled"), 16)
            act.wait_ge(sem("evacuated"), 2)
            act.dma_start(mv_dram, flat(mvt[:, :, :])).then_inc(sem("mkv_spilled"), 16)
            act.wait_ge(sem("mkv_spilled"), 32)
            act.wait_ge(sem("a1_ready"), 2)

            def p_hi(g):
                act.wait_ge(sem("dft_t"), g + 1)
                if g >= 2:
                    act.wait_ge(sem("dft_d"), g - 1)
                for dt in range(2):
                    kt = 2 * g + dt
                    src = ps[:, 4 + 2 * (g % 2) + dt, :]
                    A(pdft[:, g % 2, dt, 0, 1:S], src[:, 1:S], ACT.Identity, scale=a1[:, kt:kt + 1])
                    last = A(pdft[:, g % 2, dt, 0, S:2 * S], src[:, S:2 * S], ACT.Identity, scale=na1[:, kt:kt + 1])
                last.then_inc(sem("p_hi"), 1)
                act.wait_ge(sem("dc_ready"), g + 1)
                A(pdft[:, g % 2, :, 0, 0:1].rearrange("p a b -> p (a b)"), dc[:, :], ACT.Copy).then_inc(sem("dc_hi"), 1)

            def fm_hi(g):
                act.wait_ge(sem("dft_d"), g + 1)
                A(xt[:, 2 * g:2 * g + 2, 0, :], ps[:, g % 2, :].rearrange("p (a b) -> p a b", a=2),
                  ACT.Copy).then_inc(sem("fm_hi"), 1)

            p_hi(0)
            for g in range(8):
                if g < 7:
                    p_hi(g + 1)
                fm_hi(g)
            for g in range(GQ):
                for m in range(CH * (G_FN + g) + (4 if g else 0), CH * (G_FN + g + 1) + (4 if g < GQ - 1 else 0)):
                    hi_static(m)
                act.wait_ge(sem("chunk_used"), CH * (G_FN + g + 1))
                for a in range(HALVES):
                    A(tmp[:, 0:2, :].rearrange("p a b -> p (a b)"), ps[:, 2 * (g % 2) + a, :], ACT.Square,
                      accum_out=ssq[:, a, g:g + 1]).then_inc(sem("sq"), 1)
                    act.wait_ge(sem("sq"), 5 + 2 * g + a)
            root(3)

            def h_squares(n0):
                for n in range(4):
                    a, b = divmod(n, 2)
                    act.wait_ge(sem("h_piece"), n0 + n + 1)
                    A(flat(tmp[:, :, :]), h[:, a, b * 1024:(b + 1) * 1024], ACT.Square,
                      accum_out=ssq[:, a, b:b + 1]).then_inc(sem("hsq"), 1)
                    act.wait_ge(sem("hsq"), n0 + n + 1)

            h_squares(0)
            root(4)
            act.wait_ge(sem("a2_ready"), 1)
            for r in range(4):
                act.wait_ge(sem("turned"), 4 + r + 1)
                for j in range(4):
                    kt = 4 * r + j
                    last = A(x1t[:, kt, :], ps[:, 4 + 2 * (r % 2) + j // 2, (j % 2) * S:(j % 2 + 1) * S], ACT.Copy,
                             scale=a2[:, kt:kt + 1])
                last.then_inc(sem("x1t_out"), 1)
            act.wait_ge(sem("x1t_out"), 4)
            for r in range(4):
                act.wait_ge(sem("a2_ready"), 2 + r // 2)
                for j in range(4):
                    kt = 4 * r + j
                    last = A(xt[:, kt, 0, :], x1t[:, kt, :], ACT.Identity, bias=s2[:, kt:kt + 1])
                last.then_inc(sem("xt_hi"), 1)
                if r == 1:
                    hi_static(CH * G_ML1)
                    hi_static(CH * G_ML1 + 1)
                if r > 1:
                    hi_static(CH * G_ML1 + r)

            def mlp_quarter(G0, ups, q, last=False):
                with act.Fori(0, 2) as p:
                    for e in range(2):
                        hi_run(q * 64 + p * 16 + (CH * (G0 + e) + 4))
                        act.wait_ge(sem("chunk_used"), q * 64 + p * 16 + CH * (G0 + e + 1))
                        b0 = 4 * ((G0 + e) % 2)
                        A(tmp[:, :, :], ps[:, b0:b0 + 4, S:2 * S], ACT.Copy).then_inc(sem("up_lo"), 1)
                        act.wait_ge(sem("up_sq"), q * 4 + p * 2 + (ups + e + 1))
                        A(u[:, bass.ds(p * 8 + 4 * e, 4), 0, :], tmp[:, :, :], ACT.Copy).then_inc(sem("u_hi"), 1)

                def down(p, e, final=False):
                    m0 = q * 64 + p * 16 + (CH * (G0 + 4 + e) + 4)
                    if final:
                        for j in range(4):
                            hi(4 + j, (j % RAW, (m0 + (C_OFF + RAW)) * 4), m0 + (j - CH + 1))
                    else:
                        hi_run(m0)
                    if ups == 0:
                        act.wait_ge(sem("evacuated"), q * 8 + p * 2 + (G0 + 4 + e + 1))
                        for a in range(HALVES):
                            A(tmp[:, 2 * a:2 * a + 2, :].rearrange("p a b -> p (a b)"),
                              y[:, a, bass.ds(p * 1024 + e * GC, GC)], ACT.Square,
                              accum_out=ssq[:, a, bass.ds(p * 2 + e, 1)]).then_inc(sem("ysq"), 1)

                if last:
                    for p in range(2):
                        for e in range(2):
                            down(p, e, final=ups > 0 and p == 1 and e == 1)
                else:
                    with act.Fori(0, 2) as p:
                        for e in range(2):
                            down(p, e)

            with act.Fori(0, QT - 1) as q:
                mlp_quarter(G_ML1, 0, q)
            mlp_quarter(G_ML1, 0, QT - 1, last=True)
            root(5)
            h_squares(4)
            root(6)
            act.wait_ge(sem("narrow_in"), 48)
            xt_hi(2, v("attn", KT))
            A(wsh[:, :, :], wsr[:, :, :], ACT.Copy).then_inc(sem("ws_hi"), 1)

            def lvl_exp(n):
                act.wait_ge(sem("lvl_d"), n + 1)
                A(eg[:, :, :], eg[:, :, :], ACT.Exp, scale=1.0 / GLA_TAU).then_inc(sem("lvl_e"), 1)

            def square(name, dst, src, ready, value=1):
                act.wait_ge(sem(ready), value)
                A(dst, src, ACT.Square).then_inc(sem(name + "_sq"), 1)

            def head_roots(*norms):
                for name, dst, b0, banks in norms:
                    act.wait_ge(sem(name + "_mm"), 1)
                    A(flat(dst[:, :, :]).rearrange("p (b n) -> p b n", b=banks), ps[:, b0:b0 + banks, :], ACT.Ln,
                      bias=eps[:, 0:1], scale=1.0 / P).then_inc(sem(name + "_ln"), 1)
                for name, dst, b0, banks in norms:
                    act.wait_ge(sem(name + "_ln"), 1)
                    A(dst[:, :, :], dst[:, :, :], ACT.Exp, scale=-0.5).then_inc(sem(name + "_root"), 1)

            def soft_exp(name, pr):
                act.wait_ge(sem(name + "_max"), 1)
                for j in range(8):
                    A(pr[:, j, :], pr[:, j, :], ACT.Exp, bias=nmx[:, j:j + 1],
                      accum_out=sm[:, j:j + 1]).then_inc(sem(name + "_e"), 1)

            def gate_steps(k):
                G, n = G_WIN + k, k - 7

                def step(j):
                    if j == 0:
                        if k == 9:
                            head_roots(("fo", fosq, 4, 2))
                        act.wait_ge(sem("chunk_used"), CH * G + CH)
                        A(flat(gt[:, :, :]).rearrange("p (b n) -> p b n", b=2), ps[:, 2 * (G % 2):2 * (G % 2) + 2, :],
                          ACT.Abs).then_inc(sem("gate_abs"), 1)
                        act.wait_ge(sem("gate_abs"), n)
                        A(gt[:, :, :], gt[:, :, :], ACT.Exp, scale=-1.0).then_inc(sem("gate_e"), 1)
                    if j == 1:
                        act.wait_ge(sem("gate_e"), n)
                        A(gt[:, :, :], gt[:, :, :], ACT.Ln, bias=1.0).then_inc(sem("gate_ln"), 1)
                    if j == 2:
                        act.wait_ge(sem("gate_log"), n)
                        A(gt[:, :, :], gt[:, :, :], ACT.Exp).then_inc(sem("gate_s"), 1)
                    if j == 3:
                        act.wait_ge(sem("evacuated"), G + 1)
                        A(u[:, 4 * (k - 8):4 * (k - 7), 0, :], gt[:, :, :], ACT.Copy).then_inc(sem("z_hi"), 1)
                return step

            for k in range(len(WIN_GROUPS)):
                G = G_WIN + k
                hi_run(CH * G + 4, gate_steps(k - 1) if k >= 9 else None)
                if k == 0:
                    act.wait_ge(sem("z_neg"), 2)
                    for t in (eg[:, :, :], fft[32:36, :]):
                        A(t, t, ACT.Exp).then_inc(sem("z_exp"), 1)
                    act.wait_ge(sem("z_exp"), 2)
                    for t in (eg[:, :, :], fft[32:36, :]):
                        A(t, t, ACT.Ln, bias=1.0).then_inc(sem("z_ln"), 1)
                if 2 <= k <= 5:
                    lvl_exp(2 * (k - 2) + 1)
                if k == 7:
                    head_roots(("o", osq, 4, 4))
                if k == 8:
                    soft_exp("fox", pf)
                if k == 9:
                    head_roots(("mq", tmp, 6, 2))
                    square("fo", fosq[:, :, :], ot[:, 8:12, :], "fo_out")
                if k == 10:
                    soft_exp("mem", pm)
                if k == 11:
                    square("mo", tmp[:, :, :], ot[:, 12:16, :], "mo_out")
                    head_roots(("mo", tmp, 6, 2))
                if 1 <= k <= 4:
                    lvl_exp(2 * (k - 1))
                if k == 6:
                    square("o", osq[:, :, :], ot[:, 0:8, :], "gla_out")
                    square("fq", fqsq[:, :, :], fq[:, :, :], "evacuated", G_WIN + 5)
                    square("fk", fksq[:, :, :], fk[:, :, :], "evacuated", G_WIN + 6)
                if k == 7:
                    square("mq", tmp[:, :, :], mq[:, :, :], "evacuated", G_WIN + 8)
                    head_roots(("fq", fqsq, 4, 2), ("fk", fksq, 6, 2))
            for g in range(GQ):
                hi_run(CH * (G_WO + g) + 4, gate_steps(len(WIN_GROUPS) - 1) if g == 0 else None)
                act.wait_ge(sem("evacuated"), G_WO + g + 1)
                for a in range(HALVES):
                    A(tmp[:, 2 * a:2 * a + 2, :].rearrange("p a b -> p (a b)"), h[:, a, g * GC:(g + 1) * GC], ACT.Square,
                      accum_out=ssq[:, a, g:g + 1]).then_inc(sem("osqs"), 1)
            root(7)
            xt_hi(3, v("mlp", KT))
            with act.Fori(0, QT - 1) as q:
                mlp_quarter(G_ML2, 4 * QT, q)
            mlp_quarter(G_ML2, 4 * QT, QT - 1, last=True)

        @block.vector
        def _(dve):
            V = nc.vector
            steps = [0]

            def link(ins):
                steps[0] += 1
                ins.then_inc(sem("dve_step"), 1)
                dve.wait_ge(sem("dve_step"), steps[0])

            def lo(i, s, hi_value):
                dve.wait_ge(sem("w_hi"), hi_value)
                V.tensor_tensor(flat(wl[:, i, :, :]), raw[:, s, :], flat(wh[:, i, :, :]).bitcast(F32),
                                ALU.subtract).then_inc(sem(f"raw_used{s}"), 1)

            def lo_static(m):
                lo(m % CH, chunk_c(m) % RAW, m + 1)

            def lo_run(m0, between=None):
                for j in range(CH):
                    if between:
                        between(j)
                    lo((4 + j) % CH, j % RAW, m0 + (j + 1))

            summed = {}

            def gemv(vec, c0, n, a):
                if n in PE_MOD.get(vec, []):
                    return
                kt, half = mod_part(vec, n)
                s, r = slot_of(mod_c(c0, n))
                dve.wait_ge(sem(f"raw_landed{s}"), 16 * r)
                if (vec, half) in summed:
                    s0, r0 = summed[vec, half]
                    dve.wait_ge(sem(f"raw_used{s0}"), r0)
                summed[vec, half] = (s, r)
                t = (acc[0], acc[1], acc2)[a][:, half * MODC:(half + 1) * MODC]
                V.scalar_tensor_tensor(out=t, in0=raw[:, s, :], scalar=siluc[:, kt:kt + 1], in1=t,
                                       op0=ALU.mult, op1=ALU.add).then_inc(sem(f"raw_used{s}"), 1)

            def mean(parts, n, done, value):
                dve.wait_ge(sem(done), value)
                V.tensor_reduce(ssm[:, :], ssq[:, :, 0:parts], AX.X, ALU.add).then_inc(sem("ssm_ready"), 1)
                dve.wait_ge(sem("rooted"), n)
                V.reciprocal(rstd[:, :], srt[:, :]).then_inc(sem("rs_ready"), 1)
                dve.wait_ge(sem("rs_ready"), n)

            def diagonals():
                for a in range(HALVES):
                    V.tensor_scalar(dg[:, a, :], ident[:, :], rstd[:, a:a + 1], None, ALU.mult).then_inc(sem("dg_ready"), 1)

            def xt_lo_round(build, r, gain):
                dve.wait_ge(sem("xt_hi"), 4 * build + r + 1)
                for j in range(4):
                    kt = 4 * r + j
                    last = V.scalar_tensor_tensor(out=xt[:, kt, 1, :], in0=ps[:, 4 + 2 * (r % 2) + j // 2, (j % 2) * S:(j % 2 + 1) * S],
                                                  scalar=gain[:, kt:kt + 1], in1=xt[:, kt, 0, :].bitcast(F32),
                                                  op0=ALU.mult, op1=ALU.subtract)
                last.then_inc(sem("xt_ready"), 1)

            def mod_vector(n, dst, bank):
                dve.wait_ge(sem("mod_mm"), n)
                V.tensor_copy(dst, ps[:, bank, 0:KT]).then_inc(sem("mod_out"), 1)
                dve.wait_ge(sem("mod_out"), n)

            dve.wait_ge(sem("vt_mm"), 1)
            link(V.tensor_copy(vt[:, :], ps[:, 0, 0:VROWS]))
            link(V.tensor_scalar(v("fqg"), v("fqg"), float(P) ** -0.5, None, ALU.mult))
            V.tensor_scalar(v("mqg"), v("mqg"), float(P) ** -0.5, None, ALU.mult).then_inc(sem("vt_ready"), 1)
            dve.wait_ge(sem("c_exp"), 1)
            link(V.tensor_scalar(vtmp[:, :], vtmp[:, :], 1.0, None, ALU.add))
            link(V.reciprocal(vtmp[:, :], vtmp[:, :]))
            V.tensor_tensor(siluc[:, :], v("c", KT), vtmp[:, :], ALU.mult).then_inc(sem("silu_ready"), 1)
            dve.wait_ge(sem("silu_ready"), 1)
            mean(1, 1, "sq", 2)
            diagonals()
            dve.wait_ge(sem("acc0_seeded"), 16)
            for n in range(MODN):
                if n in (6, 8, 10, 12):
                    xt_lo_round(0, (n - 6) // 2, v("mem", KT))
                if n == 16:
                    mean(1, 2, "sq", 4)
                if n == 20:
                    dve.wait_ge(sem("dft_hi"), 1)
                    V.tensor_copy(flat(lmask[:, :, :]), lmask_raw[:, :])
                    V.tensor_tensor(dftl[:, :, :], dft_raw[:, :, :], dfth[:, :, :].bitcast(F32),
                                    ALU.subtract).then_inc(sem("dft_lo"), 1)
                if n in (24, 28):
                    a = (n - 24) // 4
                    dve.wait_ge(sem("xn_hi"), a + 1)
                    V.scalar_tensor_tensor(out=xn[:, 1, a, :], in0=h[:, a, :], scalar=rstd[:, a:a + 1],
                                           in1=xn[:, 0, a, :].bitcast(F32), op0=ALU.mult,
                                           op1=ALU.subtract).then_inc(sem("xn_lo"), 1)
                gemv("sc1", C_SC1, n, 0)
            dve.wait_ge(sem("acc1_seeded"), 16)
            for m in range(2 * CH):
                lo_static(m)
                for j in range(2):
                    gemv("sh1", C_MEM, 2 * m + j, 1)
                if m == 2:
                    mod_vector(1, vtmp[:, :], 2)
                    link(V.tensor_scalar(vtmp[:, :], vtmp[:, :], 1.0, None, ALU.add))
                    link(V.tensor_tensor(a1[:, :], v("ng0", KT), vtmp[:, :], ALU.mult))
                    V.tensor_scalar(na1[:, :], a1[:, :], -1.0, None, ALU.mult).then_inc(sem("a1_ready"), 1)
            dve.wait_ge(sem("mk_root"), 1)
            dve.wait_ge(sem("evacuated"), 1)
            V.scalar_tensor_tensor(out=mkt[:, :, :], in0=mkt[:, :, :], scalar=v("mkg"), in1=mksq[:, :, :],
                                   op0=ALU.mult, op1=ALU.mult).then_inc(sem("mk_normed"), 1)
            dve.wait_ge(sem("acc0_seeded"), 32)
            for n in range(2):
                gemv("g1", C_G1, n, 0)
            mod_vector(2, vtmp[:, :], 7)
            V.tensor_scalar(s1[:, :], vtmp[:, :], float(S), None, ALU.mult).then_inc(sem("a1_ready"), 1)
            dve.wait_ge(sem("a1_ready"), 2)

            def p_lo(g):
                dve.wait_ge(sem("p_hi"), g + 1)
                if g:
                    dve.wait_ge(sem("p_lo"), g)
                for dt in range(2):
                    kt = 2 * g + dt
                    last = V.tensor_scalar(dc[:, dt:dt + 1], ps[:, 4 + 2 * (g % 2) + dt, 0:1], a1[:, kt:kt + 1],
                                           s1[:, kt:kt + 1], ALU.mult, ALU.add)
                last.then_inc(sem("dc_ready"), 1)
                for dt in range(2):
                    kt = 2 * g + dt
                    for o, n, t in ((1, S, a1), (S, 2 * S, na1)):
                        V.scalar_tensor_tensor(out=pdft[:, g % 2, dt, 1, o:n], in0=ps[:, 4 + 2 * (g % 2) + dt, o:n],
                                               scalar=t[:, kt:kt + 1], in1=pdft[:, g % 2, dt, 0, o:n].bitcast(F32),
                                               op0=ALU.mult, op1=ALU.subtract)
                dve.wait_ge(sem("dc_hi"), g + 1)
                V.tensor_tensor(pdft[:, g % 2, :, 1, 0:1].rearrange("p a b -> p (a b)"), dc[:, :],
                                pdft[:, g % 2, :, 0, 0:1].rearrange("p a b -> p (a b)").bitcast(F32),
                                ALU.subtract).then_inc(sem("p_lo"), 1)

            for n in range(2, 4):
                gemv("g1", C_G1, n, 0)
            p_lo(0)

            def fm_lo(g):
                dve.wait_ge(sem("fm_hi"), g + 1)
                V.tensor_tensor(xt[:, 2 * g:2 * g + 2, 1, :], ps[:, g % 2, :].rearrange("p (a b) -> p a b", a=2),
                                xt[:, 2 * g:2 * g + 2, 0, :].bitcast(F32), ALU.subtract).then_inc(sem("fm_lo"), 1)

            for g in range(8):
                if g:
                    for n in range(4 * g, 4 * g + 4):
                        gemv("g1", C_G1, n, 0)
                if g < 7:
                    p_lo(g + 1)
                fm_lo(g)
            dve.wait_ge(sem("acc1_seeded"), 32)

            def gate(k, banks, slot0, halves=(0, 1)):
                dve.wait_ge(sem("gate_mm"), k + 1)
                for half in halves:
                    dve.wait_ge(sem("slot_in"), 16 * (slot0 + half + 1))
                    t = acc[0][:, half * MODC:(half + 1) * MODC].rearrange("p (b n) -> p b n", b=2)
                    V.tensor_tensor(t, ps[:, banks[half]:banks[half] + 2, :],
                                    slot[:, :].rearrange("p (b n) -> p b n", b=2), ALU.mult).then_inc(sem("slot_used"), 1)
                    dve.wait_ge(sem("slot_used"), slot0 + half + 1)

            def y_block(g):
                for a in range(HALVES):
                    dve.wait_ge(sem("sq"), 5 + 2 * g + a)
                    last = V.tensor_tensor(y[:, a, g * GC:(g + 1) * GC], ps[:, 2 * (g % 2) + a, :],
                                           acc[0][:, g * GC:(g + 1) * GC], ALU.mult)
                last.then_inc(sem("evacuated"), 1)

            for g in range(GQ):
                G = G_FN + g
                for i in range(CH):
                    lo_static(CH * G + i)
                    gemv("sc2", C_FN, CH * g + i, 1)
                    if g == 0 and i in (4, 6):
                        gate(0, (4, 6), 0, ((i - 4) // 2,))
                    if g and i == 3:
                        y_block(g - 1)

            def residual(n):
                a, b = divmod(n, 2)
                cols = slice(b * 1024, (b + 1) * 1024)
                V.scalar_tensor_tensor(out=h[:, a, cols], in0=y[:, a, cols], scalar=rstd[:, a:a + 1],
                                       in1=h[:, a, cols], op0=ALU.mult, op1=ALU.add).then_inc(sem("h_piece"), 1)

            dve.wait_ge(sem("acc2_seeded"), 16)

            def shift_half(half):
                dve.wait_ge(sem("mod_mm"), 4 + half)
                k8 = slice(8 * half, 8 * half + 8)
                V.tensor_copy(s2[:, k8], ps[:, 7 * half, k8]).then_inc(sem("a2_ready"), 1)
                dve.wait_ge(sem("a2_ready"), 2 + half)

            def shifted_lo(r):
                dve.wait_ge(sem("x1t_out"), r + 1)
                dve.wait_ge(sem("xt_hi"), 4 + r + 1)
                for j in range(4):
                    kt = 4 * r + j
                    last = V.scalar_tensor_tensor(out=xt[:, kt, 1, :], in0=x1t[:, kt, :], scalar=s2[:, kt:kt + 1],
                                                  in1=xt[:, kt, 0, :].bitcast(F32), op0=ALU.add, op1=ALU.subtract)
                last.then_inc(sem("xt_ready"), 1)

            for n in range(MODN):
                if n == 1:
                    y_block(GQ - 1)
                    mean(4, 3, "sq", 12)
                    dve.wait_ge(sem("evacuated"), G_ML1)
                    for piece in range(4):
                        residual(piece)
                if n == 3:
                    mod_vector(3, vtmp[:, :], 7)
                    link(V.tensor_scalar(vtmp[:, :], vtmp[:, :], 1.0, None, ALU.add))
                    V.tensor_tensor(a2[:, :], v("ng2", KT), vtmp[:, :], ALU.mult).then_inc(sem("a2_ready"), 1)
                if n == 4:
                    mean(2, 4, "hsq", 4)
                    diagonals()
                if n == 18:
                    shift_half(0)
                if n in (21, 26):
                    shifted_lo((n - 21) // 5)
                gemv("sh2", C_SH2, n, 2)
            lo_static(CH * G_ML1)
            shift_half(1)
            lo_static(CH * G_ML1 + 1)
            for r in (2, 3):
                shifted_lo(r)
                lo_static(CH * G_ML1 + r)

            def mlp_quarter(G0, ups, q, side, onto, last=False):
                def side_chunk(p, e, down):
                    n = q * 8 + p * 2 + (e + 4 * down)
                    dve.wait_ge(sem("slot_in"), n * 16 + 48)
                    dve.wait_ge(sem("slot_used"), n + 1)
                    t = acc[0][:, e * MODC:(e + 1) * MODC]
                    V.scalar_tensor_tensor(out=t, in0=slot[:, :], scalar=siluc[:, bass.ds(q * 4 + p + 2 * down, 1)], in1=t,
                                           op0=ALU.mult, op1=ALU.add).then_inc(sem("slot_used"), 1)

                with dve.Fori(0, 2) as p:
                    for e in range(2):
                        lo_run(q * 64 + p * 16 + (CH * (G0 + e) + 4))
                        if side:
                            side_chunk(p, e, 0)
                        n, b0 = q * 4 + p * 2 + (ups + e), 4 * ((G0 + e) % 2)
                        dve.wait_ge(sem("up_lo"), n + 1)
                        V.tensor_tensor(tmp[:, :, :], ps[:, b0:b0 + 4, 0:S], tmp[:, :, :], ALU.add).then_inc(sem("evacuated"), 1)
                        dve.wait_ge(sem("evacuated"), q * 8 + p * 2 + (G0 + e + 1))
                        V.scalar_tensor_tensor(out=tmp[:, :, :], in0=tmp[:, :, :], scalar=0.0, in1=tmp[:, :, :],
                                               op0=ALU.max, op1=ALU.mult).then_inc(sem("up_sq"), 1)
                        dve.wait_ge(sem("u_hi"), n + 1)
                        w = bass.ds(p * 8 + 4 * e, 4)
                        V.tensor_tensor(u[:, w, 1, :], tmp[:, :, :], u[:, w, 0, :].bitcast(F32),
                                        ALU.subtract).then_inc(sem("u_lo"), 1)

                def gate_and_products(j):
                    if j != 6:
                        return
                    gate(1, (2, 6), 2 + MODN)
                    for g in range(GQ - 1):
                        dve.wait_ge(sem("ysq"), 8 * (QT - 1) + 2 * (g + 1))
                        gated(g)

                def down(p, e, tail=False):
                    m0 = q * 64 + p * 16 + (CH * (G0 + 4 + e) + 4)
                    early = side and last and p == 1
                    if early and e == 0:
                        side_chunk(1, 0, 1)
                    if tail and not side:
                        for j in range(4):
                            lo(4 + j, j % RAW, m0 + (j + 1))
                    else:
                        lo_run(m0, gate_and_products if tail else None)
                    if early and e == 0:
                        side_chunk(1, 1, 1)
                    elif side and not early:
                        side_chunk(p, e, 1)
                    dve.wait_ge(sem("chunk_used"), q * 64 + p * 16 + CH * (G0 + 4 + e + 1))
                    b0 = 4 * ((G0 + e) % 2)
                    cols = bass.ds(p * 1024 + e * GC, GC)
                    V.tensor_tensor(onto[:, :, cols], onto[:, :, cols], ps[:, b0:b0 + 2, :], ALU.add).then_inc(sem("evacuated"), 1)

                if last:
                    for p in range(2):
                        for e in range(2):
                            down(p, e, tail=p == 1 and e == 1)
                else:
                    with dve.Fori(0, 2) as p:
                        for e in range(2):
                            down(p, e)

            def gated(g):
                t = y[:, :, g * GC:(g + 1) * GC]
                V.tensor_tensor(t, t, acc[0][:, g * GC:(g + 1) * GC].rearrange("p (o n) -> p o n", o=1)
                                .to_broadcast([P, HALVES, GC]), ALU.mult).then_inc(sem("y_gated"), 1)

            dve.wait_ge(sem("acc0_seeded"), 48)
            dve.wait_ge(sem("y_zero"), 1)
            with dve.Fori(0, QT - 1) as q:
                mlp_quarter(G_ML1, 0, q, True, y)
            mlp_quarter(G_ML1, 0, QT - 1, True, y, last=True)
            dve.wait_ge(sem("ysq"), 8 * QT)
            gated(GQ - 1)
            mean(4, 5, "ysq", 8 * QT)
            dve.wait_ge(sem("y_gated"), GQ)
            for n in range(4):
                residual(n)
            mean(2, 6, "hsq", 8)
            diagonals()
            for r in range(4):
                xt_lo_round(2, r, v("attn", KT))
            dve.wait_ge(sem("ws_hi"), 1)
            V.tensor_tensor(wsl[:, :, :], wsr[:, :, :], wsh[:, :, :].bitcast(F32), ALU.subtract).then_inc(sem("ws_lo"), 1)

            def banks(t, n=2):
                return flat(t).rearrange("p (b n) -> p b n", b=n)

            def scale_heads(t, gains, root, tiles):
                for j in range(tiles):
                    last = V.scalar_tensor_tensor(out=t[:, j, :], in0=t[:, j, :], scalar=gains(j), in1=root[:, j, :],
                                                  op0=ALU.mult, op1=ALU.mult)
                return last

            def lvl_parts(t, n):
                b = flat(t[:, :, :]).rearrange("p (n two m) -> p n two m", two=2, m=LEVELS[n])
                return b[:, :, 0, :], b[:, :, 1, :]

            def lvl_pre(n):
                m = LEVELS[n]
                b1, b2 = lvl_parts(bg, n)
                ref = b1[:, :, m - 1:m].to_broadcast([P, 512 // m, m])
                eq, ek = (flat(eg[:, 2 * i:2 * i + 2, :]).rearrange("p (n m) -> p n m", m=m) for i in range(2))
                if n == 0:
                    V.tensor_copy(eq, b2)
                else:
                    V.tensor_tensor(eq, b2, ref, ALU.subtract)
                V.tensor_tensor(ek, ref, b1, ALU.subtract).then_inc(sem("lvl_d"), 1)
                dve.wait_ge(sem("lvl_e"), n + 1)
                V.tensor_tensor(lvl_parts(qd, n)[1], eq, lvl_parts(qg, n)[1], ALU.mult)
                V.tensor_tensor(lvl_parts(kd, n)[0], ek, lvl_parts(kg, n)[0], ALU.mult).then_inc(sem("lvl_ready"), 1)

            def lvl_post(n):
                dve.wait_ge(sem("lvl_mm"), n + 1)
                if n == 0:
                    V.tensor_copy(banks(soff[:, :, :]), ps[:, 4:6, :]).then_inc(sem("lvl_out"), 1)
                else:
                    V.copy_predicated(sd[:, :, :], lmask[:, n - 1:n, :].to_broadcast([P, 16, P]),
                                      ps[:, 4:8, :].rearrange("p b (t n) -> p (b t) n", t=4)).then_inc(sem("lvl_out"), 1)

            def soft(name, pr, masked):
                dve.wait_ge(sem(name + "_qk"), 1)
                src, dst = ps[:, 4:8, :], banks(pr[:, :, :], 4)
                if masked:
                    link(V.tensor_tensor(dst, src, flat(mask[:, :, :]).rearrange("p (o n) -> p o n", o=1)
                                         .to_broadcast([P, 4, 2 * S]), ALU.add))
                else:
                    link(V.tensor_copy(dst, src))
                link(V.tensor_reduce(mx[:, :], pr[:, :, :], AX.X, ALU.max))
                V.tensor_scalar(nmx[:, :], mx[:, :], -1.0, None, ALU.mult).then_inc(sem(name + "_max"), 1)
                dve.wait_ge(sem(name + "_e"), 8)
                link(V.reciprocal(rs[:, :], sm[:, :]))
                for j in range(8):
                    last = V.tensor_scalar(pr[:, j, :], pr[:, j, :], rs[:, j:j + 1], None, ALU.mult)
                last.then_inc(sem(name + "_p"), 1)

            dve.wait_ge(sem("narrow_mm"), 1)
            V.tensor_copy(gat[0:16, :], ps[0:16, 4, 0:S]).then_inc(sem("gat_ready"), 1)
            V.tensor_scalar(ffz[32:36, :], ps[32:36, 4, 0:S], foxb[32:36, 0:1], None, ALU.add).then_inc(sem("gat_ready"), 1)
            fvv = flat(fv[:, :, :]).rearrange("p (a n) -> p a n", a=HALVES)
            into = dict(gk=kg, fq=fq, fk=fk, mq=mq)

            def gate_steps(k):
                G, n = G_WIN + k, k - 8
                src, g2d = ps[:, 2 * (G % 2):2 * (G % 2) + 2, :], banks(gt[:, :, :])

                def step(j):
                    if j == 1:
                        dve.wait_ge(sem("gate_ln"), n + 1)
                        V.scalar_tensor_tensor(out=g2d, in0=src, scalar=0.0, in1=g2d, op0=ALU.min,
                                               op1=ALU.subtract).then_inc(sem("gate_log"), 1)
                    if j == 2:
                        dve.wait_ge(sem("gate_s"), n + 1)
                        if WIN_GROUPS[k][0] == "gg":
                            link(V.tensor_tensor(g2d, src, g2d, ALU.mult))
                        V.tensor_tensor(gt[:, :, :], gt[:, :, :], ot[:, 4 * n:4 * n + 4, :], ALU.mult).then_inc(sem("evacuated"), 1)
                    if j == 3:
                        dve.wait_ge(sem("z_hi"), n + 1)
                        V.tensor_tensor(u[:, 4 * n:4 * n + 4, 1, :], gt[:, :, :], u[:, 4 * n:4 * n + 4, 0, :].bitcast(F32),
                                        ALU.subtract).then_inc(sem("z_lo"), 1)
                        if k in (8, 10):
                            name = "fox" if k == 8 else "mem"
                            dve.wait_ge(sem(name + "_turn"), 1)
                            V.tensor_copy(pt[:, :, :, :].rearrange("p h a s -> p h (a s)"), ps[:, 4:8, :]).then_inc(sem(name + "_pt"), 1)
                        if k == 9:
                            dve.wait_ge(sem("fo_root"), 1)
                            link(scale_heads(ot[:, 8:12, :], lambda j: v("out", 1, 8 + j), fosq[:, :, :], 4))
                return step

            for k, (name, off) in enumerate(WIN_GROUPS):
                G = G_WIN + k
                lo_run(CH * G + 4, gate_steps(k - 1) if k >= 9 else None)
                if k == 0:
                    dve.wait_ge(sem("la_mm"), 1)
                    for j in range(4):
                        last = V.tensor_scalar(bg[:, j, :], ps[:, 4 + j // 2, (j % 2) * S:(j % 2 + 1) * S], v("gab", 1, j),
                                               None, ALU.add)
                    link(last)
                    dve.wait_ge(sem("gat_ready"), 2)
                    for z, t in ((bg[:, :, :], eg[:, :, :]), (ffz[32:36, :], fft[32:36, :])):
                        V.scalar_tensor_tensor(out=t, in0=z, scalar=-1.0, in1=z, op0=ALU.mult, op1=ALU.min).then_inc(sem("z_neg"), 1)
                if 2 <= k <= 5:
                    lvl_post(2 * (k - 2))
                    lvl_pre(2 * (k - 2) + 1)
                if k == 6:
                    lvl_post(8)
                if k == 7:
                    dve.wait_ge(sem("o_root"), 1)
                    link(scale_heads(ot, lambda j: v("out", 1, j), osq[:, :, :], 8))
                if k == 8:
                    soft("fox", pf, True)
                if k == 9:
                    dve.wait_ge(sem("fox_pv"), 1)
                    V.tensor_copy(banks(ot[:, 8:12, :]), ps[:, 4:6, :]).then_inc(sem("fo_out"), 1)
                    dve.wait_ge(sem("mq_root"), 1)
                    scale_heads(mq, lambda j: v("mqg"), tmp[:, :, :], 4).then_inc(sem("mem_qk_ready"), 1)
                    dve.wait_ge(sem("mem_qk_ready"), 1)
                if k == 10:
                    soft("mem", pm, False)
                if k == 11:
                    dve.wait_ge(sem("mem_pv"), 1)
                    V.tensor_copy(banks(ot[:, 12:16, :]), ps[:, 4:6, :]).then_inc(sem("mo_out"), 1)
                    dve.wait_ge(sem("mo_root"), 1)
                    link(scale_heads(ot[:, 12:16, :], lambda j: v("out", 1, 12 + j), tmp[:, :, :], 4))
                if k >= 8:
                    continue
                dve.wait_ge(sem("chunk_used"), CH * G + CH)
                src = ps[:, 2 * (G % 2):2 * (G % 2) + 2, :]
                if name == "gq":
                    V.tensor_scalar(banks(qg[:, :, :]), src, float(64) ** -0.5, None, ALU.mult).then_inc(sem("evacuated"), 1)
                elif name in into:
                    if k == 4:
                        dve.wait_ge(sem("h_spilled"), 16)
                    V.tensor_copy(banks(into[name][:, :, :]), src).then_inc(sem("evacuated"), 1)
                elif name == "gv":
                    V.tensor_copy(gv[:, :, off:off + GC], src).then_inc(sem("evacuated"), 1)
                elif name == "fv":
                    V.tensor_copy(fvv, src).then_inc(sem("evacuated"), 1)
                if k == 0:
                    dve.wait_ge(sem("z_ln"), 2)
                    for z, t in ((bg[:, :, :], eg[:, :, :]), (ffz[32:36, :], fft[32:36, :])):
                        link(V.scalar_tensor_tensor(out=t, in0=z, scalar=0.0, in1=t, op0=ALU.min, op1=ALU.subtract))
                    for j in range(4):
                        for tb in range(HALVES):
                            r = slice(tb * P, (tb + 1) * P)
                            last = V.tensor_tensor_scan(bg[:, j, r], ones[:, :], eg[:, j, r], 0.0, ALU.mult, ALU.add)
                    link(last)
                    link(V.tensor_tensor_scan(fc[32:36, 0:P], ones[32:36, :], fft[32:36, 0:P], 0.0, ALU.mult, ALU.add))
                    V.tensor_tensor_scan(fc[32:36, P:S], ones[32:36, :], fft[32:36, P:S], fc[32:36, P - 1:P],
                                         ALU.mult, ALU.add).then_inc(sem("fc_ready"), 1)
                if k == 1:
                    dve.wait_ge(sem("gla_zero"), 3)
                    lvl_pre(0)
                if 2 <= k <= 5:
                    lvl_post(2 * (k - 2) + 1)
                    if k <= 4:
                        lvl_pre(2 * (k - 1))
                if k == 6:
                    dve.wait_ge(sem("gla_mm"), 1)
                    V.tensor_copy(banks(ot[:, 0:8, :], 4), ps[:, 4:8, :]).then_inc(sem("gla_out"), 1)
                if k == 7:
                    dve.wait_ge(sem("fq_root"), 1)
                    dve.wait_ge(sem("fk_root"), 1)
                    link(scale_heads(fq, lambda j: v("fqg"), fqsq[:, :, :], 4))
                    scale_heads(fk, lambda j: v("fkg"), fksq[:, :, :], 4).then_inc(sem("fox_qk_ready"), 1)

            for g in range(GQ):
                G = G_WO + g
                lo_run(CH * G + 4, gate_steps(len(WIN_GROUPS) - 1) if g == 0 else None)
                dve.wait_ge(sem("chunk_used"), CH * (G + 1))
                if g == 0:
                    dve.wait_ge(sem("h_back"), 16)
                cols = slice(g * GC, (g + 1) * GC)
                V.tensor_tensor(h[:, :, cols], h[:, :, cols], ps[:, 2 * (G % 2):2 * (G % 2) + 2, :],
                                ALU.add).then_inc(sem("evacuated"), 1)
            mean(4, 7, "osqs", 8)
            diagonals()
            for r in range(4):
                xt_lo_round(3, r, v("mlp", KT))
            with dve.Fori(0, QT - 1) as q:
                mlp_quarter(G_ML2, 4 * QT, q, False, h)
            mlp_quarter(G_ML2, 4 * QT, QT - 1, False, h, last=True)


WIN_GROUPS = [("gq", 0), ("gk", 0), ("gv", 0), ("gv", GC), ("fq", 0), ("fk", 0), ("fv", 0), ("mq", 0),
              ("gg", 0), ("gg", GC), ("fg", 0), ("mg", 0)]
N_ROWS = 13
N_CONSTS = 4
SH2_TURN = 6

_INS = ["x", "c", "w_mod", "b_mod", "norm_g", "w_mlp_in", "w_mlp_out", "fnet_w_out", "mem_2", "attn_norm_g_2", "w_in_2",
        "gla_a_w2_2", "gla_a_b_2", "fox_f_b_2", "fox_q_norm_g_2", "fox_k_norm_g_2", "mem_norm_g_2", "w_mem_kv_2",
        "mem_q_norm_g_2", "mem_k_norm_g_2", "out_norm_g_2", "w_out_2", "mlp_norm_g_2", "w_up_2", "w_down_2"]


def shape_constants():
    n = np.arange(S)
    angle = 2 * np.pi * (np.outer(n, n) % S) / S
    i = np.arange(P)
    masks = [((i[None, :] // (2 * m) == i[:, None] // (2 * m)) & (i[None, :] % (2 * m) >= m) & (i[:, None] % (2 * m) < m))
             if m else i[None, :] == i[:, None] for m in LEVELS[1:]]
    keys = np.arange(S)
    causal = [np.where(keys[None, :] <= (tb * P + i)[:, None], 0.0, NEG) for tb in range(HALVES)]
    return {
        "k_ident": np.eye(P, dtype=np.float32),
        "k_dft": np.concatenate([np.cos(angle), np.sin(angle)], 1).astype(np.float32),
        "k_mask": np.concatenate(causal, 1).astype(np.float32),
        "k_nsel": np.repeat(-np.eye(4, dtype=np.float32), P, axis=1),
        "k_sel": np.eye(4, dtype=np.float32),
        "k_levels": np.concatenate(masks, 1).astype(np.float32),
    }


def kernel(**inputs):
    import numpy as _np
    import concourse.bacc as _bacc
    from concourse import mybir as _mybir
    from concourse.bass_utils import run_bass_kernel_spmd as _run

    nc = _bacc.Bacc("TRN2", target_bir_lowering=False, num_devices=1)
    arrays, args = {}, []
    for name, a in [(n, inputs[n]) for n in _INS] + list(shape_constants().items()):
        a = _np.ascontiguousarray(a)
        arrays[f"in_{name}_dram"] = a
        args.append(nc.dram_tensor(f"in_{name}_dram", a.shape, _mybir.dt.from_np(a.dtype), kind="ExternalInput").ap())
    args.append(nc.dram_tensor("out_0_dram", (1, S, D), F32, kind="ExternalOutput").ap())
    program(nc, *args)
    r = _run(nc, [arrays], core_ids=[0])
    return r.results[0]["out_0_dram"]
```
